# Optimizing a Trainium2 kernel written in Bass

```python
import jax, jax.numpy as jnp
from jax import lax
import numpy as np

D_MODEL = 1024
BATCH = 1
SEQ = 1024
DEPTH = 1

D_MIX = D_MODEL
HEAD_DIM = 64
NSA_HEADS = 8
NSA_KV_HEADS = 2
NSA_GROUP = NSA_HEADS // NSA_KV_HEADS
D_NSA = NSA_HEADS * HEAD_DIM
D_KV = NSA_KV_HEADS * HEAD_DIM
D_CONV = D_MIX - D_NSA
CONV_GROUPS = D_CONV // HEAD_DIM
CONV_WIDTH = 3
N_BRANCH = 3
ROPE_THETA = 500000.0
ROT_DIM = HEAD_DIM // 4
CMP_LEN = 32
CMP_STRIDE = 16
CMP_HIDDEN = 2 * HEAD_DIM
SEL_BLOCK = 64
SEL_TOPK = 16
WINDOW = 512
Q_BLOCK = 64
EPS = 1e-6
NEG_INF = -1e30
FORCE_SCORE = 1e9
SPLIT_SIZES = (D_NSA, 6 * D_KV, N_BRANCH * NSA_HEADS, D_NSA, D_CONV, D_CONV, D_CONV, D_CONV)
D_IN = sum(SPLIT_SIZES)
SPLIT_POINTS = tuple(int(v) for v in np.cumsum(SPLIT_SIZES)[:-1])

kernel_name = "hybrid_nsa_shortconv_layer"

def rms_norm(x, w):
    xf = x.astype(jnp.float32)
    xf = xf * lax.rsqrt(jnp.mean(xf * xf, axis=-1, keepdims=True) + EPS)
    return (xf * w.astype(jnp.float32)).astype(x.dtype)

def apply_rope(x, pos):
    inv_freq = ROPE_THETA ** (-jnp.arange(0, ROT_DIM, 2, dtype=jnp.float32) / ROT_DIM)
    ang = pos.astype(jnp.float32)[:, None] * inv_freq[None, :]
    cos = jnp.cos(ang)[:, None, :]
    sin = jnp.sin(ang)[:, None, :]
    xr = x[..., :ROT_DIM].astype(jnp.float32)
    x1, x2 = xr[..., :ROT_DIM // 2], xr[..., ROT_DIM // 2:]
    rot = jnp.concatenate([x1 * cos - x2 * sin, x2 * cos + x1 * sin], axis=-1)
    return jnp.concatenate([rot.astype(x.dtype), x[..., ROT_DIM:]], axis=-1)

def masked_softmax(s, mask):
    p = jax.nn.softmax(jnp.where(mask, s, NEG_INF), axis=-1)
    return jnp.where(mask, p, 0.0)

def compress_blocks(kv, pos_emb, w1, b1, w2):
    B_, S_, G_, dh = kv.shape
    halves = kv.reshape(B_, S_ // CMP_STRIDE, CMP_STRIDE, G_, dh)
    blocks = jnp.concatenate([halves[:, :-1], halves[:, 1:]], axis=2)
    blocks = blocks + pos_emb[None, None, :, None, :]
    nc = blocks.shape[1]
    flat = jnp.moveaxis(blocks, 3, 2).reshape(B_, nc, G_, CMP_LEN * dh)
    hid = jax.nn.silu(jnp.einsum('bcgf,fh->bcgh', flat, w1) + b1)
    return jnp.einsum('bcgh,hd->bcgd', hid, w2)

def cmp_sel_overlap(nc, ns):
    cs = jnp.arange(nc) * CMP_STRIDE
    ce = cs + CMP_LEN
    ss = jnp.arange(ns) * SEL_BLOCK
    se = ss + SEL_BLOCK
    ov = jnp.clip(jnp.minimum(ce[:, None], se[None, :]) - jnp.maximum(cs[:, None], ss[None, :]), 0)
    return ov.astype(jnp.float32) / CMP_LEN

def hybrid_layer(x, norm_w, w_in, q_norm_w, k_norm_w, cmp_k_pos, cmp_k_w1, cmp_k_b1, cmp_k_w2,
                 cmp_v_pos, cmp_v_w1, cmp_v_b1, cmp_v_w2, conv_w, conv_b, w_out):
    B_, S_, _ = x.shape
    G, R, dh = NSA_KV_HEADS, NSA_GROUP, HEAD_DIM
    nc = S_ // CMP_STRIDE - 1
    ns = S_ // SEL_BLOCK
    n_sel = min(SEL_TOPK, ns)
    nqb = S_ // Q_BLOCK

    h = rms_norm(x, norm_w)
    proj = jnp.einsum('bsd,de->bse', h, w_in)
    q, kv_all, gate_logits, nsa_z, cv_h, cv_b, cv_c, cv_z = jnp.split(proj, SPLIT_POINTS, axis=-1)

    pos = jnp.arange(S_)
    q = apply_rope(rms_norm(q.reshape(B_, S_, NSA_HEADS, dh), q_norm_w), pos)
    k_c, v_c, k_s, v_s, k_w, v_w = [t.reshape(B_, S_, G, dh) for t in jnp.split(kv_all, 6, axis=-1)]
    cmp_end = jnp.arange(nc) * CMP_STRIDE + (CMP_LEN - 1)
    k_c = apply_rope(rms_norm(compress_blocks(k_c, cmp_k_pos, cmp_k_w1, cmp_k_b1, cmp_k_w2),
                              k_norm_w[0]), cmp_end)
    v_c = compress_blocks(v_c, cmp_v_pos, cmp_v_w1, cmp_v_b1, cmp_v_w2)
    k_s = apply_rope(rms_norm(k_s, k_norm_w[1]), pos)
    k_w = apply_rope(rms_norm(k_w, k_norm_w[2]), pos)
    k_sel_blk = k_s.reshape(B_, ns, SEL_BLOCK, G, dh).transpose(0, 3, 1, 2, 4)
    v_sel_blk = v_s.reshape(B_, ns, SEL_BLOCK, G, dh).transpose(0, 3, 1, 2, 4)
    pad = ((0, 0), (WINDOW, 0), (0, 0), (0, 0))
    k_w_pad = jnp.pad(k_w, pad)
    v_w_pad = jnp.pad(v_w, pad)
    overlap = cmp_sel_overlap(nc, ns)
    scale = HEAD_DIM ** -0.5
    b_ix = jnp.arange(B_)[:, None, None, None]
    g_ix = jnp.arange(G)[None, :, None, None]
    blk = jnp.arange(ns)
    tok_in_blk = jnp.arange(SEL_BLOCK)
    win_off = jnp.arange(Q_BLOCK + WINDOW)

    def query_block(args):
        qb, i = args
        t = i * Q_BLOCK + jnp.arange(Q_BLOCK)
        s_c = jnp.einsum('bgqrd,bcgd->bgqrc', qb, k_c).astype(jnp.float32) * scale
        p_c = masked_softmax(s_c, (cmp_end[None, :] <= t[:, None])[None, None, :, None, :])
        o_cmp = jnp.einsum('bgqrc,bcgd->bgqrd', p_c.astype(v_c.dtype), v_c)
        imp = jnp.einsum('bgqrc,cn->bgqn', p_c, overlap)
        cur = t[:, None] // SEL_BLOCK
        forced = (blk[None, :] == 0) | (blk[None, :] == cur) | (blk[None, :] == cur - 1)
        visible = blk[None, :] * SEL_BLOCK <= t[:, None]
        imp = jnp.where(forced, FORCE_SCORE, jnp.where(visible, imp, -1.0))
        _, idx = lax.top_k(imp, n_sel)
        k_g = k_sel_blk[b_ix, g_ix, idx]
        v_g = v_sel_blk[b_ix, g_ix, idx]
        s_s = jnp.einsum('bgqrd,bgqnld->bgqrnl', qb, k_g).astype(jnp.float32) * scale
        tok = idx[..., None] * SEL_BLOCK + tok_in_blk
        mask_s = tok <= t[None, None, :, None, None]
        n_tok = n_sel * SEL_BLOCK
        p_s = masked_softmax(s_s.reshape(B_, G, Q_BLOCK, R, n_tok),
                             mask_s.reshape(B_, G, Q_BLOCK, 1, n_tok))
        o_slc = jnp.einsum('bgqrm,bgqmd->bgqrd', p_s.astype(v_g.dtype),
                           v_g.reshape(B_, G, Q_BLOCK, n_tok, dh))
        start = i * Q_BLOCK
        k_wb = lax.dynamic_slice_in_dim(k_w_pad, start, Q_BLOCK + WINDOW, axis=1)
        v_wb = lax.dynamic_slice_in_dim(v_w_pad, start, Q_BLOCK + WINDOW, axis=1)
        key_pos = start - WINDOW + win_off
        mask_w = ((key_pos[None, :] <= t[:, None]) & (key_pos[None, :] > t[:, None] - WINDOW)
                  & (key_pos[None, :] >= 0))
        s_w = jnp.einsum('bgqrd,bkgd->bgqrk', qb, k_wb).astype(jnp.float32) * scale
        p_w = masked_softmax(s_w, mask_w[None, None, :, None, :])
        o_win = jnp.einsum('bgqrk,bkgd->bgqrd', p_w.astype(v_wb.dtype), v_wb)
        return o_cmp, o_slc, o_win

    q_blocks = q.reshape(B_, nqb, Q_BLOCK, G, R, dh).transpose(1, 0, 3, 2, 4, 5)
    o_cmp, o_slc, o_win = lax.map(query_block, (q_blocks, jnp.arange(nqb)))

    def unblock(o):
        return o.transpose(1, 0, 3, 2, 4, 5).reshape(B_, S_, NSA_HEADS, dh)

    gates = jax.nn.sigmoid(gate_logits.astype(jnp.float32)).astype(x.dtype)
    gates = gates.reshape(B_, S_, NSA_HEADS, N_BRANCH)
    o_nsa = (gates[..., 0:1] * unblock(o_cmp) + gates[..., 1:2] * unblock(o_slc)
             + gates[..., 2:3] * unblock(o_win))
    o_nsa = o_nsa.reshape(B_, S_, D_NSA) * jax.nn.silu(nsa_z)

    u = cv_c * cv_h
    conv = lax.conv_general_dilated(u, conv_w[:, None, :], window_strides=(1,),
                                    padding=[(CONV_WIDTH - 1, 0)],
                                    dimension_numbers=('NWC', 'WIO', 'NWC'),
                                    feature_group_count=D_CONV) + conv_b
    o_conv = cv_b * conv * jax.nn.silu(cv_z)

    mix = jnp.concatenate([o_nsa, o_conv], axis=-1)
    return x + jnp.einsum('bse,ed->bsd', mix, w_out)

def setup_inputs(seed: int = 0) -> dict:
    key = jax.random.key(seed)
    ks = jax.random.split(key, 17)
    L = DEPTH

    def nrm(k, shape, scale):
        return jax.random.normal(k, shape, jnp.float32) * scale

    f_in = CMP_LEN * HEAD_DIM
    return {
        "x": nrm(ks[0], (BATCH, SEQ, D_MODEL), 1.0),
        "norm_w": 1.0 + nrm(ks[1], (L, D_MODEL), 0.01),
        "w_in": nrm(ks[2], (L, D_MODEL, D_IN), D_MODEL ** -0.5),
        "q_norm_w": 1.0 + nrm(ks[3], (L, HEAD_DIM), 0.01),
        "k_norm_w": 1.0 + nrm(ks[4], (L, N_BRANCH, HEAD_DIM), 0.01),
        "cmp_k_pos": nrm(ks[5], (L, CMP_LEN, HEAD_DIM), 0.02),
        "cmp_k_w1": nrm(ks[6], (L, f_in, CMP_HIDDEN), f_in ** -0.5),
        "cmp_k_b1": nrm(ks[7], (L, CMP_HIDDEN), 0.01),
        "cmp_k_w2": nrm(ks[8], (L, CMP_HIDDEN, HEAD_DIM), CMP_HIDDEN ** -0.5),
        "cmp_v_pos": nrm(ks[9], (L, CMP_LEN, HEAD_DIM), 0.02),
        "cmp_v_w1": nrm(ks[10], (L, f_in, CMP_HIDDEN), f_in ** -0.5),
        "cmp_v_b1": nrm(ks[11], (L, CMP_HIDDEN), 0.01),
        "cmp_v_w2": nrm(ks[12], (L, CMP_HIDDEN, HEAD_DIM), CMP_HIDDEN ** -0.5),
        "conv_w": nrm(ks[13], (L, CONV_WIDTH, D_CONV), CONV_WIDTH ** -0.5),
        "conv_b": nrm(ks[14], (L, D_CONV), 0.01),
        "w_out": nrm(ks[15], (L, D_MIX, D_MODEL), D_MIX ** -0.5),
    }

def reference(x, norm_w, w_in, q_norm_w, k_norm_w, cmp_k_pos, cmp_k_w1, cmp_k_b1, cmp_k_w2,
              cmp_v_pos, cmp_v_w1, cmp_v_b1, cmp_v_w2, conv_w, conv_b, w_out):
    for l in range(DEPTH):
        x = hybrid_layer(x, norm_w[l], w_in[l], q_norm_w[l], k_norm_w[l], cmp_k_pos[l],
                         cmp_k_w1[l], cmp_k_b1[l], cmp_k_w2[l], cmp_v_pos[l], cmp_v_w1[l],
                         cmp_v_b1[l], cmp_v_w2[l], conv_w[l], conv_b[l], w_out[l])
    return x


_drawn_inputs = setup_inputs


def setup_inputs(seed=0):
    import zlib

    import numpy as np

    out = dict(_drawn_inputs(seed))
    spreads = {}
    factors = {'norm_w': 6.551,
     'q_norm_w': 64.0,
     'k_norm_w': 64.0,
     'cmp_k_pos': 64.0,
     'cmp_k_b1': 64.0,
     'cmp_v_pos': 64.0,
     'cmp_v_b1': 200.0,
     'conv_b': 200.0,
     'cmp_k_w1': 7.113,
     'cmp_k_w2': 7.083,
     'cmp_v_w1': 6.85,
     'cmp_v_w2': 5.699}
    for name, (base, spread) in spreads.items():
        noise = np.random.default_rng([zlib.crc32(name.encode()), seed]).standard_normal(out[name].shape)
        drawn = base * np.exp(spread * noise) if base else spread * noise
        out[name] = __import__('jax').numpy.asarray(drawn.astype(out[name].dtype))
    for name, factor in factors.items():
        out[name] = (out[name] * factor).astype(out[name].dtype)
    return out
```

```python
from contextlib import ExitStack

import numpy as np

import concourse.bass as bass
from concourse import mybir

F32 = mybir.dt.float32
F32R = mybir.dt.float32r
ALU = mybir.AluOpType
ACT = mybir.ActivationFunctionType
AX = mybir.AxisListType

P = 128
SEQ = 1024
DM = 1024
NT = SEQ // P
NK = DM // P
HD = 64
HEADS, GROUPS = 8, 2
GH = HEADS // GROUPS
ROT = 8
CMP_STRIDE, CMP_LEN = 16, 32
CB = SEQ // CMP_STRIDE
WIN = 512
WT = WIN // P
EPS = 1e-6
NEG = -1e30
assert SEQ // 64 <= 16, "every selection block is among the top 16"

ENTRIES = [("q", 0, 256, 0), ("kc", 512, 256, 0), ("q", 256, 256, 1), ("w1", 0, 256, 0),
           ("kv", 768, 256, 0), ("w1", 1, 256, 1), ("kv", 1024, 280, 1),
           ("z", 1304, 256, 0), ("z", 1560, 256, 1)]
for pair in range(2):
    for kind, col in (("ch", 1816), ("cc", 2840), ("cb", 2328), ("cz", 3352)):
        ENTRIES.append((kind, col + 256 * pair, 256, pair))
NE = len(ENTRIES)
ITEMS = {"q": NT, "kv": NT, "w1": 0}
OFFS = [0]
for _, _, w, _ in ENTRIES:
    OFFS.append(OFFS[-1] + NK * w)

C_ID, C_CAUSAL, C_FAR, C_CMP = 0, 128, 256, 384
C_COS, C_SIN, C_COSC, C_SINC, C_VALID, C_EPS, NC_ = 504, 568, 632, 640, 648, 649, 650
P_CW, P_CB, P_B1, P_POS, P_W2, NPAR = 0, 12, 16, 18, 50, 178


def items_of(e):
    return ITEMS.get(ENTRIES[e][0], 4)


UNITS = [(i, g) for i in reversed(range(NT)) for g in range(GROUPS)]
NJ = 2 * len(UNITS)
LAST_W = NJ + 5


def job_tiles(n):
    i, _ = UNITS[n // 2]
    if n % 2 == 0:
        return [("s", j) for j in range(i + 1)]
    return [("w", j) for j in range(max(0, i - WT), i + 1)] + [("c", 0)]


def quarter(n, h):
    t = job_tiles(n)
    return t[len(t) * h // 4:len(t) * (h + 1) // 4]


def q_prep_at(w, h):
    u = (w + 1) // 2
    return u if h == 3 and w % 2 == 1 and u < len(UNITS) else None


def out_part(w, h):
    a = 4 * w + h - 1 - 4 * 5
    if a < 0 or a // 16 >= NT:
        return None
    return NT - 1 - a // 16, a % 16


def transposes_until():
    tp, pt, at, pv = 1, 0, {}, {}
    for w in range(NJ + 1):
        for h in range(4):
            if q_prep_at(w, h) is not None:
                tp += 1
            if w >= 1:
                tp += len(quarter(w - 1, h))
                pt += len(quarter(w - 1, h))
        at[w - 1], pv[w - 1] = tp, pt
    return at, pv


def hybrid_layer(nc: bass.Bass, x, wpack, wout, normw, qnorm, knorm, par, const, out):
    with ExitStack() as ctx:
        def sb(name, shape, dt=F32, c=ctx):
            return c.enter_context(nc.sbuf_tensor(name, shape, dt))

        cst = sb("cst", [P, NC_])
        masks = sb("masks", [P, 504], F32R)
        gate = sb("gate", [P, NT, 3 * HEADS])
        kcmp = sb("kcmp", [P, P], F32R)
        vcmp = sb("vcmp", [CB, GROUPS, P], F32R)
        nmax = sb("nmax", [P, 4, 2])
        psums = sb("psums", [P, 4, 2])
        precip = sb("precip", [P, 4, 2])
        qn = sb("qn", [P, NT, HEADS * HD])
        kst = sb("kst", [P, 2, GROUPS, SEQ], F32R)
        val = sb("val", [P, 2, NT, GROUPS, P], F32R)
        mixn = sb("mixn", [P, 4, SEQ])
        with ExitStack() as c:
            xch = sb("xch", [P, 16, P], F32R, c)
            xcl = sb("xcl", [P, 16, P], F32R, c)
        mixc = sb("mixc", [P, 4, SEQ])

        with ExitStack() as c:
            hh = sb("hh", [P, NK, SEQ], F32R, c)
            hl = sb("hl", [P, NK, SEQ], F32R, c)
            raw = [sb(f"raw{s}", [P, 560], F32, c) for s in range(4)]
            wh = [sb(f"wh{s}", [P, NK * (280 - 24 * s)], F32R, c) for s in range(2)]
            wl = [sb(f"wl{s}", [P, NK * (280 - 24 * s)], F32R, c) for s in range(2)]
            ub = sb("ub", [P, 2 * (SEQ + 2)], F32, c)
            sq = sb("sq", [P, 512], F32, c)
            hdh = sb("hdh", [P, P], F32R, c)
            hdl = sb("hdl", [P, P], F32R, c)
            prm = sb("prm", [P, NPAR], F32, c)
            hnorm = sb("hnorm", [P, 4, HD], F32, c)
            w2h = sb("w2h", [P, 2, HD], F32R, c)
            w2l = sb("w2l", [P, 2, HD], F32R, c)
            stat = sb("stat", [P, 5, 48], F32, c)
        with ExitStack() as c:
            woh = sb("woh", [P, NK, DM], F32R, c)
            wol = sb("wol", [P, NK, DM], F32R, c)
            p_sel = sb("p_sel", [P, GH, SEQ], F32, c)
            p_win = sb("p_win", [P, GH, 704], F32, c)
            pth = [sb(f"pth{s}", [P, 512], F32R, c) for s in range(2)]
            ptl = [sb(f"ptl{s}", [P, 512], F32R, c) for s in range(2)]
            qh = sb("qh", [P, GH, P], F32R, c)
            ql = sb("ql", [P, GH, P], F32R, c)
            qd = sb("qd", [P, GH, 2, HD], F32, c)
            ot = sb("ot", [P, 2, P], F32, c)
            xo = [sb(f"xo{s}", [P, 512], F32, c) for s in range(2)]
            with ExitStack() as d:
                wor = [sb(f"wor{s}", [P, DM], F32, d) for s in range(2)]
            msh = sb("msh", [P, NK, P], F32R, c)
            msl = sb("msl", [P, NK, P], F32R, c)

        with ExitStack() as c:
            pj = [c.enter_context(nc.psum_tensor(f"pj{s}", [P, 512], F32)) for s in range(4)]
            xt = [c.enter_context(nc.psum_tensor(f"xt{s}", [P, 512], F32)) for s in range(4)]
        with ExitStack() as c:
            sc = [c.enter_context(nc.psum_tensor(f"sc{s}", [P, 1024], F32)) for s in range(2)]
            tp = [c.enter_context(nc.psum_tensor(f"tp{s}", [P, 512], F32)) for s in range(2)]
            po = c.enter_context(nc.psum_tensor("po", [P, 512], F32))
            pout = c.enter_context(nc.psum_tensor("pout", [P, 512], F32))

        def sem(name):
            return ctx.enter_context(nc.semaphore(name))

        const_in, param_in, normw_in = sem("const_in"), sem("param_in"), sem("normw_in")
        x_in = [sem(f"x_in{s}") for s in range(2)]
        raw_in = [sem(f"raw_in{s}") for s in range(4)]
        masks_ready, w2_hi, w2_ready = sem("masks_ready"), sem("w2_hi"), sem("w2_ready")
        x_sq, x_std, x_norm = sem("x_sq"), sem("x_std"), sem("x_norm")
        xt_done, hh_ready, hl_ready = sem("xt_done"), sem("hh_ready"), sem("hl_ready")
        wh_ready, wl_ready = sem("wh_ready"), sem("wl_ready")
        item_done, act_rel, dve_rel = sem("item_done"), sem("act_rel"), sem("dve_rel")
        sq_ready, sq_read = sem("sq_ready"), sem("sq_read")
        head_std = sem("head_std")
        th_ready, cz_done, q_normed = sem("th_ready"), sem("cz_done"), sem("q_normed")
        blocks_ready, xch_ready, xcl_ready = sem("blocks_ready"), sem("xch_ready"), sem("xcl_ready")
        hid_done, hid_pre, hid_tanh, hid_act = sem("hid_done"), sem("hid_pre"), sem("hid_tanh"), sem("hid_act")
        hdh_ready, hdl_ready, cmp_done = sem("hdh_ready"), sem("hdl_ready"), sem("cmp_done")
        ck_raw, ck_std, cv_hi, cv_ready = sem("ck_raw"), sem("ck_std"), sem("cv_hi"), sem("cv_ready")
        ck_sum = sem("ck_sum")
        keys_normed, kt_done, kt_hi, kt_ready = sem("keys_normed"), sem("kt_done"), sem("kt_hi"), sem("kt_ready")
        gate_raw, gate_tanh = sem("gate_raw"), sem("gate_tanh")
        dve_chain = sem("dve_chain")
        wor_in = [sem(f"wor_in{s}") for s in range(2)]
        woh_ready, wol_ready = sem("woh_ready"), sem("wol_ready")
        qd_ready, qh_ready = sem("qd_ready"), sem("qh_ready")
        s_done, max_ready, exp_done, p_ready = sem("s_done"), sem("max_ready"), sem("exp_done"), sem("p_ready")
        tp_done, tp_read, pth_ready, ptl_ready = sem("tp_done"), sem("tp_read"), sem("pth_ready"), sem("ptl_ready")
        pv_done, ot_copied, o_read, mix_ready = sem("pv_done"), sem("ot_copied"), sem("o_read"), sem("mix_ready")
        msh_ready, msl_ready = sem("msh_ready"), sem("msl_ready")
        out_done, out_ready = sem("out_done"), sem("out_ready")
        xo_in = [sem(f"xo_in{s}") for s in range(2)]
        stored = [sem(f"stored{s}") for s in range(2)]

        ident = cst[:, C_ID:C_ID + P]
        identr = masks[:, C_ID:C_ID + P]
        tiles = lambda ap, t: ap[:, t * P:(t + 1) * P]
        xtile = lambda t: ub[:, (t % 2) * SEQ:(t % 2 + 1) * SEQ]
        krow = ub[:, 0:SEQ * 2].rearrange("p (t g u d) -> p t g u d", t=NT, g=GROUPS, u=2)
        ubuf = ub[:, :].rearrange("p (f s) -> p f s", f=2)
        blocks = [mixn[:, 2 * f:2 * f + 2, :] for f in range(2)]
        hid = mixn[:, 0, 0:4 * P].rearrange("p (a c) -> p a c", a=4)
        ckr = mixn[:, 1, 0:2 * HD].rearrange("p (u d) -> p u d", u=2)
        cksq = mixn[:, 1, 2 * HD:3 * HD]
        cktmp = mixn[:, 1, 256:288].rearrange("p (a r) -> p a r", a=4)
        tp_end, pv_end = transposes_until()
        first_item = [sum(items_of(a) for a in range(e)) for e in range(NE + 1)]
        releases, ra, rd = [], 0, 0
        kind_of = [kind for kind, *_ in ENTRIES for _ in range(ITEMS.get(kind, 4))]
        for kind, *_ in ENTRIES:
            for _ in range(ITEMS.get(kind, 4)):
                ra += kind in ("q", "kv", "kc", "ch")
                rd += kind in ("kv", "kc", "z", "cc", "cb", "cz")
                releases.append((ra, rd))

        def entry_through(eng, e):
            if ENTRIES[e][0] == "w1":
                eng.wait_ge(hid_done, ENTRIES[e][3] + 1)
            else:
                eng.wait_ge(item_done, first_item[e + 1])

        def wait_phase_a(eng):
            entry_through(eng, NE - 1)
            eng.wait_ge(th_ready, kind_of.count("z") + kind_of.count("cz"))
            eng.wait_ge(cz_done, kind_of.count("cz"))

        block = ctx.enter_context(nc.Block())

        @block.sync
        def _(sp):
            sp.dma_start(xtile(0), x[0:P, :]).then_inc(x_in[0], 16)
            sp.dma_start(cst[:, :], const).then_inc(const_in, 16)
            sp.dma_start(mixc[:, 0, :], normw.to_broadcast([P, DM])).then_inc(normw_in, 16)
            sp.dma_start(xtile(1), x[P:2 * P, :]).then_inc(x_in[1], 16)

            def weights(p):
                e, j = divmod(p, 4)
                w = 2 * ENTRIES[e][2]
                if p >= 4:
                    sp.wait_ge(wh_ready, p - 3)
                    sp.wait_ge(wl_ready, p - 3)
                sp.dma_start(raw[p % 4][:, 0:w], wpack[:, OFFS[e] + j * w:OFFS[e] + (j + 1) * w])\
                    .then_inc(raw_in[p % 4], 16)

            for p in range(4):
                weights(p)
            sp.dma_start(prm[:, :], par).then_inc(param_in, 16)
            sp.dma_start(hnorm[:, 0, :], qnorm.to_broadcast([P, HD])).then_inc(param_in, 16)
            for b in range(3):
                sp.dma_start(hnorm[:, 1 + b, :], knorm[b:b + 1, :].to_broadcast([P, HD])).then_inc(param_in, 16)
            for t in range(2, NT):
                sp.wait_ge(xt_done, 2 * (t - 2) + 2)
                sp.dma_start(xtile(t), x[t * P:(t + 1) * P, :]).then_inc(x_in[t % 2], 16)
                if t == 4:
                    for p in range(4, 8):
                        weights(p)
            for p in range(8, 4 * NE):
                weights(p)

            wait_phase_a(sp)

            def residual(c):
                i, n = NT - 1 - c // 2, c % 2
                sp.dma_start(xo[c % 2][:, :], x[i * P:(i + 1) * P, n * 512:(n + 1) * 512]).then_inc(xo_in[c % 2], 16)

            for k in range(NK):
                if k >= 2:
                    sp.wait_ge(woh_ready, k - 1)
                    sp.wait_ge(wol_ready, k - 1)
                sp.dma_start(wor[k % 2][:, :], wout[k * P:(k + 1) * P, :]).then_inc(wor_in[k % 2], 16)
            for c in range(2):
                residual(c)
            for c in range(2 * NT):
                i, n = NT - 1 - c // 2, c % 2
                sp.wait_ge(out_ready, c + 1)
                sp.dma_start(out[i * P:(i + 1) * P, n * 512:(n + 1) * 512], xo[c % 2][:, :]).then_inc(stored[c % 2], 16)
                if c + 2 < 2 * NT:
                    sp.wait_ge(stored[c % 2], 16 * (c // 2 + 1))
                    residual(c + 2)
            for s in range(2):
                sp.wait_ge(stored[s], 16 * NT)

        @block.gpsimd
        def _(pool):
            def weights(p):
                e, j = divmod(p, 4)
                w = 2 * ENTRIES[e][2]
                pool.wait_ge(wh_ready, p + 1)
                nc.gpsimd.tensor_tensor(wl[e % 2][:, j * w:(j + 1) * w], raw[p % 4][:, 0:w],
                                        wh[e % 2][:, j * w:(j + 1) * w].bitcast(F32), ALU.subtract)\
                    .then_inc(wl_ready, 1)

            def block_lo(f):
                pool.wait_ge(xch_ready, f + 1)
                v = blocks[f].rearrange("p g (c l) -> p l g c", l=CMP_STRIDE)
                o = xcl[:, :, :].rearrange("p l (g c) -> p l g c", g=GROUPS)
                hi = xch[:, :, :].rearrange("p l (g c) -> p l g c", g=GROUPS).bitcast(F32)
                if f == 1:
                    pool.wait_ge(hid_done, 1)
                for g in range(GROUPS):
                    ins = nc.gpsimd.tensor_tensor(o[:, :, g], v[:, :, g], hi[:, :, g], ALU.subtract)
                ins.then_inc(xcl_ready, 1)

            for e in range(NE):
                for j in range(4):
                    weights(4 * e + j)
                if e == 2:
                    block_lo(0)
                if e == 4:
                    block_lo(1)
            for k in range(NK):
                if k == 0:
                    wait_phase_a(pool)
                pool.wait_ge(woh_ready, k + 1)
                nc.gpsimd.tensor_tensor(wol[:, k, :], wor[k % 2][:, :], woh[:, k, :].bitcast(F32), ALU.subtract)\
                    .then_inc(wol_ready, 1)
            for m in range(NT):
                i = NT - 1 - m
                pool.wait_ge(msh_ready, m + 1)
                for half, mix in ((0, mixn), (4, mixc)):
                    ins = nc.gpsimd.tensor_tensor(msl[:, half:half + 4, :], mix[:, :, i * P:(i + 1) * P],
                                                  msh[:, half:half + 4, :].bitcast(F32), ALU.subtract)
                ins.then_inc(msl_ready, 1)

        @block.scalar
        def _(act):
            A = nc.scalar.activation

            def weights(p):
                e, j = divmod(p, 4)
                if e >= NE:
                    return
                w = 2 * ENTRIES[e][2]
                act.wait_ge(raw_in[p % 4], 16 * (p // 4 + 1))
                if e >= 2:
                    entry_through(act, e - 2)
                nc.scalar.copy(wh[e % 2][:, j * w:(j + 1) * w], raw[p % 4][:, 0:w]).then_inc(wh_ready, 1)

            def item(e, m):
                kind, _, _, idx = ENTRIES[e]
                n = first_item[e] + m
                bank = pj[n % 4]
                act.wait_ge(item_done, n + 1)
                if kind in ("q", "kv"):
                    tk = n - sum(items_of(a) for a in range(e) if ENTRIES[a][0] not in ("q", "kv"))
                    w = 256 if kind == "q" else 128
                    if tk >= 2:
                        act.wait_ge(sq_read, tk - 1)
                    A(sq[:, (tk % 2) * 256:(tk % 2) * 256 + w], bank[:, 0:w], ACT.Square).then_inc(sq_ready, 1)
                    if kind == "q":
                        nc.scalar.copy(qn[:, m, idx * 256:(idx + 1) * 256], bank[:, 0:256]).then_inc(act_rel, 1)
                    else:
                        if idx == 1 and m == 0:
                            act.wait_ge(kt_done, 4)
                        if idx == 0 and m == 0:
                            act.wait_ge(q_normed, 2)
                        nc.scalar.copy(krow[:, m, :, 0, :], bank[:, 0:128].rearrange("p (g d) -> p g d", g=GROUPS))
                        nc.scalar.copy(val[:, idx, m, :, 0:HD],
                                       bank[:, 128:256].rearrange("p (g d) -> p g d", g=GROUPS)).then_inc(act_rel, 1)
                elif kind == "kc":
                    f, hf = divmod(m, 2)
                    if m == 0:
                        act.wait_ge(x_norm, NT)
                    o, s = (0, 16) if hf == 0 else (496, 0)
                    nc.scalar.copy(blocks[f][0:HD, 0, hf * 512:(hf + 1) * 512], bank[0:HD, :])
                    nc.scalar.copy(blocks[f][HD:P, 0, o:o + 512 - s], bank[0:HD, s:512]).then_inc(act_rel, 1)
                elif kind in ("z", "cz"):
                    before = [i for i in range(n) if kind_of[i] in ("z", "cz")]
                    if not before:
                        act.wait_ge(sq_read, 32)
                    elif kind_of[before[-1]] == "z":
                        act.wait_ge(dve_rel, releases[before[-1]][1])
                    else:
                        act.wait_ge(cz_done, kind_of[:n].count("cz"))
                    A(sq[:, :], bank[:, :], ACT.Tanh, scale=0.5).then_inc(th_ready, 1)
                elif kind == "ch":
                    f, hf = divmod(m, 2)
                    nc.scalar.copy(mixc[:, 2 * idx + f, hf * 512:(hf + 1) * 512], bank[:, :]).then_inc(act_rel, 1)

            def key_hi(n, dst, width=512):
                act.wait_ge(kt_done, n + 1)
                nc.scalar.copy(dst, xt[n % 2][:, 0:width]).then_inc(kt_hi, 1)

            def hidden(f):
                act.wait_ge(hid_pre, f + 1)
                A(hid[:, 1], hid[:, 0], ACT.Tanh, scale=0.5).then_inc(hid_tanh, 1)
                act.wait_ge(hid_act, f + 1)
                if f == 1:
                    act.wait_ge(cmp_done, 1)
                A(hdh[:, :], hid[:, 2], ACT.Copy, scale=0.5).then_inc(hdh_ready, 1)

            def block_hi(f):
                act.wait_ge(blocks_ready, f + 1)
                if f == 1:
                    act.wait_ge(hid_done, 1)
                v = blocks[f].rearrange("p g (c l) -> p l g c", l=CMP_STRIDE)
                o = xch[:, :, :].rearrange("p l (g c) -> p l g c", g=GROUPS)
                for g in range(GROUPS):
                    ins = nc.scalar.copy(o[:, :, g], v[:, :, g])
                ins.then_inc(xch_ready, 1)

            act.wait_ge(const_in, 16)
            nc.scalar.copy(masks[:, :], cst[:, 0:504]).then_inc(masks_ready, 1)
            for t in range(NT + 2):
                if t < NT:
                    act.wait_ge(x_in[t % 2], 16 * (t // 2 + 1))
                    A(kst[:, :, :, :].rearrange("p b g s -> p (b g s)")[:, (t % 4) * SEQ:(t % 4 + 1) * SEQ],
                      xtile(t), ACT.Square, accum_out=stat[:, 0, 32 + t:33 + t]).then_inc(x_sq, 1)
                    act.wait_ge(x_sq, t + 1)
                    A(stat[:, 1, 32 + t:33 + t], stat[:, 0, 32 + t:33 + t], ACT.Sqrt, scale=1.0 / DM,
                      bias=cst[:, C_EPS:C_EPS + 1]).then_inc(x_std, 1)
                    for p in {0: (0, 1), 1: (2, 3), 2: (), 3: ()}.get(t, (t,)):
                        weights(p)
                if 1 <= t <= NT:
                    for hf in range(2):
                        act.wait_ge(xt_done, 2 * (t - 1) + hf + 1)
                        nc.scalar.copy(hh[:, 4 * hf:4 * hf + 4, (t - 1) * P:t * P],
                                       xt[(2 * (t - 1) + hf) % 4][:, :].rearrange("p (k s) -> p k s", k=4))\
                            .then_inc(hh_ready, 1)
                if t >= 2:
                    item(0, t - 2)
            act.wait_ge(param_in, 80)
            nc.scalar.copy(w2h[:, :, :], prm[:, P_W2:P_W2 + 128].rearrange("p (f d) -> p f d", f=2)).then_inc(w2_hi, 1)

            norms = 0

            def root(count, scale=1.0 / HD):
                nonlocal norms
                norms += 1
                act.wait_ge(sq_read, 8 * norms)
                A(stat[:, 1, 0:count], stat[:, 0, 0:count], ACT.Sqrt, scale=scale,
                  bias=cst[:, C_EPS:C_EPS + 1]).then_inc(head_std, 1)

            root(32)
            for e in range(1, NE):
                kind, _, _, idx = ENTRIES[e]
                if kind == "kv" and idx == 1:
                    for n in range(4):
                        key_hi(n, kst[:, 0, n // 2, (n % 2) * 512:(n % 2 + 1) * 512])
                for m in range(items_of(e)):
                    item(e, m)
                    if m < 4:
                        weights(4 * (e + 1) + m)
                if kind == "w1":
                    for j in range(4):
                        weights(4 * (e + 1) + j)
                    hidden(idx)
                    if idx == 0:
                        block_hi(1)
                    else:
                        act.wait_ge(cmp_done, 1)
                        A(cksq, xt[3][:, 0:HD], ACT.Square).then_inc(ck_raw, 1)
                        nc.scalar.copy(ckr[:, 0, :], xt[3][:, 0:HD]).then_inc(ck_raw, 1)
                        act.wait_ge(ck_sum, 1)
                        A(stat[:, 1, 16:17], stat[:, 0, 16:17], ACT.Sqrt, scale=1.0 / HD,
                          bias=cst[:, C_EPS:C_EPS + 1]).then_inc(ck_std, 1)
                if kind == "kc":
                    block_hi(0)
                if kind == "q":
                    root(32)
                if kind == "kv":
                    root(16)
                    if idx == 1:
                        key_hi(4, kcmp[:, :], P)
                        act.wait_ge(cmp_done, 2)
                        for g in range(GROUPS):
                            ins = nc.scalar.copy(vcmp[:, g, 0:HD], xt[3][g * HD:(g + 1) * HD, 0:HD])
                        ins.then_inc(cv_hi, 1)
                        act.wait_ge(gate_raw, NT)
                        A(gate[:, :, :], gate[:, :, :], ACT.Tanh, scale=0.5).then_inc(gate_tanh, 1)
                if kind == "z" and idx == 0:
                    for n in range(4):
                        key_hi(5 + n, kst[:, 1, n // 2, (n % 2) * 512:(n % 2 + 1) * 512])

            wait_phase_a(act)
            tpn = ptn = 0

            def queries(u):
                nonlocal tpn
                act.wait_ge(tp_done, tpn + 1)
                if u >= 1:
                    act.wait_ge(s_done, 8 * u)
                nc.scalar.copy(qh[:, :, :], tp[tpn % 2][:, :].rearrange("p (h q) -> p h q", h=GH)).then_inc(qh_ready, 1)
                tpn += 1

            queries(0)
            for w in range(LAST_W + 1):
                for h in range(4):
                    if w < NJ:
                        i, g = UNITS[w // 2]
                        k = 4 * w + h
                        act.wait_ge(max_ready, k + 1)
                        if h == 0 and w >= 2:
                            act.wait_ge(tp_done, tp_end[w - 2])
                        if w % 2 == 0:
                            A(p_sel[:, h, 0:(i + 1) * P], sc[k % 2][:, 0:(i + 1) * P], ACT.Exp,
                              bias=nmax[:, k % 4, 0:1], accum_out=psums[:, k % 4, 0:1]).then_inc(exp_done, 1)
                        else:
                            n = min(i, WT) + 1
                            A(p_win[:, h, 640:704], sc[k % 2][:, 640:704], ACT.Exp,
                              bias=nmax[:, k % 4, 1:2], accum_out=psums[:, k % 4, 1:2])
                            A(p_win[:, h, 0:n * P], sc[k % 2][:, 0:n * P], ACT.Exp,
                              bias=nmax[:, k % 4, 0:1], accum_out=psums[:, k % 4, 0:1]).then_inc(exp_done, 1)
                    if w < 4 and h % 2 == 1:
                        p = 2 * w + h // 2
                        act.wait_ge(wor_in[p % 2], 16 * (p // 2 + 1))
                        nc.scalar.copy(woh[:, p, :], wor[p % 2][:, :]).then_inc(woh_ready, 1)
                    if h == 0 and w >= 5 and (w - 5) % 4 == 0 and (w - 5) // 4 < NT:
                        m = (w - 5) // 4
                        i = NT - 1 - m
                        act.wait_ge(mix_ready, 2 * m + 2)
                        act.wait_ge(wol_ready, NK)
                        act.wait_ge(out_done, 2 * m)
                        nc.scalar.copy(msh[:, 0:4, :], mixn[:, :, i * P:(i + 1) * P])
                        nc.scalar.copy(msh[:, 4:8, :], mixc[:, :, i * P:(i + 1) * P]).then_inc(msh_ready, 1)
                    u = q_prep_at(w, h)
                    if u is not None:
                        queries(u)
                    if 1 <= w <= NJ:
                        for kind, j in quarter(w - 1, h):
                            r = CB if kind == "c" else P
                            act.wait_ge(tp_done, tpn + 1)
                            if ptn >= 2:
                                act.wait_ge(pv_done, ptn - 1)
                            nc.scalar.copy(pth[ptn % 2][0:r, :], tp[tpn % 2][0:r, :]).then_inc(pth_ready, 1)
                            tpn += 1
                            ptn += 1
                if w >= 2 and w % 2 == 0 and w <= NJ:
                    u = w // 2 - 1
                    act.wait_ge(pv_done, pv_end[w - 1])
                    if u >= 1:
                        act.wait_ge(mix_ready, u)
                    o4 = po[:, :].rearrange("p (a b q) -> p a b q", a=2, b=2)
                    nc.scalar.copy(ot[0:HD, :, :], o4[HD:P, :, 0, :])
                    nc.scalar.copy(ot[HD:P, :, :], o4[0:HD, :, 1, :]).then_inc(ot_copied, 1)

        @block.vector
        def _(dve):
            V = nc.vector
            chain = 0

            def link(ins):
                nonlocal chain
                chain += 1
                ins.then_inc(dve_chain, 1)
                dve.wait_ge(dve_chain, chain)

            def inv_std(lo, n, width, ready, count):
                s = lambda r: stat[:, r, lo:lo + n]
                dve.wait_ge(ready, count)
                V.tensor_scalar(s(3), s(0), 1.0 / width, EPS, ALU.mult, ALU.add)
                link(V.reciprocal(s(2), s(1)))
                link(V.tensor_tensor(s(4), s(2), s(2), ALU.mult))
                link(V.scalar_tensor_tensor(s(4), s(4), -0.5, s(3), ALU.mult, ALU.mult))
                link(V.scalar_tensor_tensor(s(2), s(4), 1.5, s(2), ALU.add, ALU.mult))

            def rope(v, cos, sin, tmp):
                a, b = v[..., 0:ROT], v[..., ROT:2 * ROT]
                V.tensor_tensor(tmp[0], a, cos, ALU.mult)
                V.tensor_tensor(tmp[1], b, sin, ALU.mult)
                V.tensor_tensor(tmp[2], b, cos, ALU.mult)
                link(V.tensor_tensor(tmp[3], a, sin, ALU.mult))
                V.tensor_tensor(a, tmp[0], tmp[1], ALU.subtract)
                return V.tensor_tensor(b, tmp[2], tmp[3], ALU.add)

            def item(e, m):
                kind, _, _, idx = ENTRIES[e]
                n = first_item[e] + m
                bank = pj[n % 4]
                if kind in ("q", "kv"):
                    tk = n - sum(items_of(a) for a in range(e) if ENTRIES[a][0] not in ("q", "kv"))
                    nh = 4 if kind == "q" else 2
                    dve.wait_ge(sq_ready, tk + 1)
                    V.tensor_reduce(stat[:, 0, m * nh:(m + 1) * nh],
                                    sq[:, (tk % 2) * 256:(tk % 2) * 256 + nh * HD].rearrange("p (h d) -> p h d", h=nh),
                                    AX.X, ALU.add).then_inc(sq_read, 1)
                    if kind == "kv":
                        dve.wait_ge(act_rel, releases[n][0])
                        if idx == 1:
                            V.tensor_copy(gate[:, m, :], bank[:, 256:280]).then_inc(gate_raw, 1)
                        V.tensor_tensor(val[:, idx, m, :, HD:P], bank[:, 128:256].rearrange("p (g d) -> p g d", g=GROUPS),
                                        val[:, idx, m, :, 0:HD].bitcast(F32), ALU.subtract).then_inc(dve_rel, 1)
                    return
                dve.wait_ge(item_done, n + 1)
                f, hf = divmod(m, 2)
                cols = slice(hf * 512, (hf + 1) * 512)
                if kind == "kc":
                    o, s = (0, 16) if hf == 0 else (496, 0)
                    V.tensor_copy(blocks[f][0:HD, 1, cols], bank[HD:P, :])
                    V.tensor_copy(blocks[f][HD:P, 1, o:o + 512 - s], bank[HD:P, s:512]).then_inc(dve_rel, 1)
                elif kind == "z":
                    zi = sum(k in ("z", "cz") for k in kind_of[:n])
                    dve.wait_ge(th_ready, zi + 1)
                    V.scalar_tensor_tensor(mixn[:, 2 * idx + f, cols], sq[:, :], 1.0, bank[:, :], ALU.add, ALU.mult)\
                        .then_inc(dve_rel, 1)
                elif kind == "cc":
                    dve.wait_ge(act_rel, releases[n][0])
                    V.tensor_tensor(ubuf[:, f, 2 + hf * 512:2 + (hf + 1) * 512], bank[:, :],
                                    mixc[:, 2 * idx + f, cols], ALU.mult).then_inc(dve_rel, 1)
                    dve.wait_ge(dve_rel, releases[n][1])
                    if hf == 1:
                        t = 2 * idx + f
                        y = mixc[:, t, :]
                        cw = lambda k: prm[:, P_CW + 3 * t + k:P_CW + 3 * t + k + 1]
                        link(V.tensor_scalar(y, ubuf[:, f, 2:2 + SEQ], cw(2), prm[:, P_CB + t:P_CB + t + 1],
                                             ALU.mult, ALU.add))
                        link(V.scalar_tensor_tensor(y, ubuf[:, f, 1:1 + SEQ], cw(1), y, ALU.mult, ALU.add))
                        link(V.scalar_tensor_tensor(y, ubuf[:, f, 0:SEQ], cw(0), y, ALU.mult, ALU.add))
                elif kind == "cb":
                    mc = mixc[:, 2 * idx + f, cols]
                    V.tensor_tensor(mc, bank[:, :], mc, ALU.mult).then_inc(dve_rel, 1)
                elif kind == "cz":
                    zi = sum(k in ("z", "cz") for k in kind_of[:n])
                    dve.wait_ge(th_ready, zi + 1)
                    mc = mixc[:, 2 * idx + f, cols]
                    V.scalar_tensor_tensor(sq[:, :], sq[:, :], 1.0, bank[:, :], ALU.add, ALU.mult).then_inc(dve_rel, 1)
                    dve.wait_ge(dve_rel, releases[n][1])
                    V.scalar_tensor_tensor(mc, sq[:, :], 0.5, mc, ALU.mult, ALU.mult).then_inc(cz_done, 1)

            def key_lo(n, dst, width=512):
                dve.wait_ge(kt_hi, n + 1)
                V.tensor_tensor(dst, xt[n % 2][HD:P, 0:width], dst.bitcast(F32), ALU.subtract).then_inc(kt_ready, 1)

            dve.wait_ge(normw_in, 16)
            dve.wait_ge(const_in, 16)
            for t in range(NT + 2):
                if t < NT:
                    inv_std(32 + t, 1, DM, x_std, t + 1)
                    V.scalar_tensor_tensor(xtile(t), xtile(t), stat[:, 2, 32 + t:33 + t], mixc[:, 0, :], ALU.mult, ALU.mult)\
                        .then_inc(x_norm, 1)
                if 1 <= t <= NT:
                    for hf in range(2):
                        n = 2 * (t - 1) + hf
                        dve.wait_ge(hh_ready, n + 1)
                        hi = hh[:, 4 * hf:4 * hf + 4, (t - 1) * P:t * P]
                        V.tensor_tensor(hl[:, 4 * hf:4 * hf + 4, (t - 1) * P:t * P],
                                        xt[n % 4][:, :].rearrange("p (k s) -> p k s", k=4), hi.bitcast(F32),
                                        ALU.subtract).then_inc(hl_ready, 1)
                if t >= 2:
                    item(0, t - 2)
            dve.wait_ge(w2_hi, 1)
            V.tensor_tensor(w2l[:, :, :], prm[:, P_W2:P_W2 + 128].rearrange("p (f d) -> p f d", f=2),
                            w2h[:, :, :].bitcast(F32), ALU.subtract).then_inc(w2_ready, 1)
            link(V.tensor_scalar(hnorm[:, 0, :], hnorm[:, 0, :], 0.125, None, ALU.mult))
            cos = cst[:, C_COS:C_COS + 64].rearrange("p (t r) -> p t r", t=NT)
            sin = cst[:, C_SIN:C_SIN + 64].rearrange("p (t r) -> p t r", t=NT)
            norms = 0

            def normalise(v, nh, weight, tmp):
                nonlocal norms
                norms += 1
                inv_std(0, NT * nh, HD, head_std, norms)
                r = stat[:, 2, 0:NT * nh].rearrange("p (t h) -> p t h", t=NT)
                wide = [P, NT, nh, HD]
                link(V.tensor_tensor(v, v, r.unsqueeze(3).to_broadcast(wide), ALU.mult))
                link(V.tensor_tensor(v, v, hnorm[:, weight, :].unsqueeze(1).unsqueeze(1).to_broadcast(wide), ALU.mult))
                some = [P, NT, nh, ROT]
                return rope(v, cos.unsqueeze(2).to_broadcast(some), sin.unsqueeze(2).to_broadcast(some), tmp)

            def normalise_q(idx):
                v = qn[:, :, idx * 256:(idx + 1) * 256].rearrange("p t (h d) -> p t h d", h=4)
                tmp = [ub[:, 256 * k:256 * (k + 1)].rearrange("p (t h r) -> p t h r", t=NT, h=4) for k in range(4)]
                normalise(v, 4, 0, tmp).then_inc(q_normed, 1)
                dve.wait_ge(q_normed, idx + 1)

            normalise_q(0)
            for e in range(1, NE):
                kind, _, _, idx = ENTRIES[e]
                if kind == "kv" and idx == 1:
                    for n in range(4):
                        key_lo(n, kst[HD:P, 0, n // 2, (n % 2) * 512:(n % 2 + 1) * 512])
                if kind == "kc":
                    for f in range(2):
                        for g in range(GROUPS):
                            link(V.memset(blocks[f][HD:P, g, SEQ - 16:SEQ], 0.0))
                if kind == "ch" and idx == 0:
                    for f in range(2):
                        link(V.memset(ubuf[:, f, 0:2], 0.0))
                if kind != "ch":
                    for m in range(items_of(e)):
                        item(e, m)
                if kind == "kc":
                    dve.wait_ge(dve_rel, 4)
                    for f in range(2):
                        dve.wait_ge(act_rel, 8 + 2 * f + 2)
                        for g in range(GROUPS):
                            v = blocks[f][:, g, :].rearrange("p (c l) -> p c l", l=CMP_STRIDE)
                            pos = prm[:, P_POS + 16 * f:P_POS + 16 * (f + 1)].unsqueeze(1).to_broadcast([P, CB, CMP_STRIDE])
                            ins = V.tensor_tensor(v, v, pos, ALU.add)
                        ins.then_inc(blocks_ready, 1)
                if kind == "q":
                    normalise_q(idx)
                if kind == "w1":
                    dve.wait_ge(hid_done, idx + 1)
                    dve.wait_ge(xcl_ready, idx + 1)
                    V.tensor_scalar(hid[:, 0], xt[2][:, 0:P], prm[:, P_B1 + idx:P_B1 + idx + 1], None, ALU.add)\
                        .then_inc(hid_pre, 1)
                    dve.wait_ge(hid_tanh, idx + 1)
                    V.scalar_tensor_tensor(hid[:, 2], hid[:, 1], 1.0, hid[:, 0], ALU.add, ALU.mult).then_inc(hid_act, 1)
                    dve.wait_ge(hdh_ready, idx + 1)
                    V.scalar_tensor_tensor(hdl[:, :], hid[:, 2], 0.5, hdh[:, :].bitcast(F32), ALU.mult, ALU.subtract)\
                        .then_inc(hdl_ready, 1)
                    if idx == 1:
                        dve.wait_ge(ck_raw, 2)
                        V.tensor_reduce(stat[:, 0, 16:17], cksq, AX.X, ALU.add).then_inc(ck_sum, 1)
                        inv_std(16, 1, HD, ck_std, 1)
                        c = ckr[:, 0, :]
                        link(V.scalar_tensor_tensor(c, c, stat[:, 2, 16:17], hnorm[:, 1, :], ALU.mult, ALU.mult))
                        link(rope(c, cst[:, C_COSC:C_COSC + ROT], cst[:, C_SINC:C_SINC + ROT],
                                  [cktmp[:, k, :] for k in range(4)]))
                        V.tensor_copy(ckr[:, 1, :], c).then_inc(keys_normed, 1)
                if kind == "kv":
                    v = krow[:, :, :, 0, :]
                    tmp = [krow[:, :, :, 1, ROT * k:ROT * (k + 1)] for k in range(4)]
                    link(normalise(v, 2, 2 + idx, tmp))
                    for g in range(GROUPS):
                        ins = V.tensor_copy(krow[:, :, g, 1, :], krow[:, :, g, 0, :])
                    ins.then_inc(keys_normed, 1)
                    if idx == 1:
                        key_lo(4, kcmp[HD:P, :], P)
                        dve.wait_ge(cv_hi, 1)
                        for g in range(GROUPS):
                            ins = V.tensor_tensor(vcmp[:, g, HD:P], xt[3][g * HD:(g + 1) * HD, 0:HD],
                                                  vcmp[:, g, 0:HD].bitcast(F32), ALU.subtract)
                        ins.then_inc(cv_ready, 1)
                        dve.wait_ge(gate_tanh, 1)
                        link(V.tensor_scalar(gate[:, :, :], gate[:, :, :], 0.5, 0.5, ALU.mult, ALU.add))
                        g0 = gate[:, 0, :].rearrange("p (h b) -> p h b", b=3)[:, :, 0]
                        link(V.tensor_scalar(g0, g0, cst[:, C_VALID:C_VALID + 1], None, ALU.mult))
                if kind == "z" and idx == 0:
                    for n in range(4):
                        key_lo(5 + n, kst[HD:P, 1, n // 2, (n % 2) * 512:(n % 2 + 1) * 512])

            wait_phase_a(dve)
            tpn = ptn = 0

            def copy_queries(u):
                i, g = UNITS[u]
                src = qn[:, i, g * 256:(g + 1) * 256].rearrange("p (h d) -> p h d", h=GH)
                for twice in range(2):
                    ins = V.tensor_copy(qd[:, :, twice, :], src)
                ins.then_inc(qd_ready, 1)

            def queries(u):
                nonlocal tpn
                dve.wait_ge(qh_ready, u + 1)
                V.tensor_tensor(ql[:, :, :], tp[tpn % 2][:, :].rearrange("p (h q) -> p h q", h=GH),
                                qh[:, :, :].bitcast(F32), ALU.subtract).then_inc(tp_read, 1)
                tpn += 1

            def scale(k):
                w, h = divmod(k, 4)
                i, g = UNITS[w // 2]
                gt = lambda b: gate[:, i, 3 * (GH * g + h) + b:3 * (GH * g + h) + b + 1]
                dve.wait_ge(exp_done, k + 1)
                if w % 2 == 0:
                    link(V.reciprocal(precip[:, k % 4, 0:1], psums[:, k % 4, 0:1]))
                    p = p_sel[:, h, 0:(i + 1) * P]
                    V.tensor_scalar(p, p, precip[:, k % 4, 0:1], gt(1), ALU.mult, ALU.mult).then_inc(p_ready, 1)
                else:
                    link(V.reciprocal(precip[:, k % 4, :], psums[:, k % 4, :]))
                    p = p_win[:, h, 640:704]
                    V.tensor_scalar(p, p, precip[:, k % 4, 1:2], gt(0), ALU.mult, ALU.mult)
                    p = p_win[:, h, 0:(min(i, WT) + 1) * P]
                    V.tensor_scalar(p, p, precip[:, k % 4, 0:1], gt(2), ALU.mult, ALU.mult).then_inc(p_ready, 1)

            copy_queries(0)
            queries(0)
            for w in range(LAST_W + 1):
                for h in range(4):
                    k = 4 * w + h
                    if w < NJ:
                        i, g = UNITS[w // 2]
                        dve.wait_ge(s_done, k + 1)
                        if w % 2 == 0:
                            V.tensor_reduce(nmax[:, k % 4, 0:1], sc[k % 2][:, 0:(i + 1) * P], AX.X, ALU.max,
                                            negate=True).then_inc(max_ready, 1)
                        else:
                            V.tensor_reduce(nmax[:, k % 4, 1:2], sc[k % 2][:, 640:704], AX.X, ALU.max, negate=True)
                            V.tensor_reduce(nmax[:, k % 4, 0:1], sc[k % 2][:, 0:(min(i, WT) + 1) * P], AX.X, ALU.max,
                                            negate=True).then_inc(max_ready, 1)
                    if h == 0 and w % 2 == 1 and (w + 1) // 2 < len(UNITS):
                        copy_queries((w + 1) // 2)
                    part = out_part(w, h)
                    if part is not None and part[1] % 8 == 7:
                        c = 2 * (NT - 1 - part[0]) + part[1] // 8
                        dve.wait_ge(out_done, c + 1)
                        dve.wait_ge(xo_in[c % 2], 16 * (c // 2 + 1))
                        V.tensor_tensor(xo[c % 2][:, :], pout[:, :], xo[c % 2][:, :], ALU.add).then_inc(out_ready, 1)
                    if 1 <= k <= 4 * NJ:
                        scale(k - 1)
                    u = q_prep_at(w, h)
                    if u is not None:
                        queries(u)
                    if 1 <= w <= NJ:
                        for kind, j in quarter(w - 1, h):
                            r = CB if kind == "c" else P
                            dve.wait_ge(pth_ready, ptn + 1)
                            V.tensor_tensor(ptl[ptn % 2][0:r, :], tp[tpn % 2][0:r, :], pth[ptn % 2][0:r, :].bitcast(F32),
                                            ALU.subtract).then_inc(tp_read, 1)
                            tpn += 1
                            ptn += 1
                if w >= 2 and w % 2 == 0 and w <= NJ:
                    u = w // 2 - 1
                    i, g = UNITS[u]
                    o4 = po[:, :].rearrange("p (a b q) -> p a b q", a=2, b=2)
                    dve.wait_ge(ot_copied, u + 1)
                    V.tensor_tensor(ot[0:HD, :, :], o4[0:HD, :, 0, :], ot[0:HD, :, :], ALU.add)
                    V.tensor_tensor(ot[HD:P, :, :], o4[HD:P, :, 1, :], ot[HD:P, :, :], ALU.add).then_inc(o_read, 1)
                    dve.wait_ge(o_read, u + 1)
                    m = mixn[:, 2 * g:2 * g + 2, i * P:(i + 1) * P]
                    V.scalar_tensor_tensor(m, m, 0.5, ot[:, :, :], ALU.mult, ALU.mult).then_inc(mix_ready, 1)

        @block.tensor
        def _(pe):
            MM = nc.tensor.matmul

            def three(dst, lh, ll, rh, rl, start, stop):
                MM(dst, lh, rh, start=start, stop=False)
                MM(dst, lh, rl, start=False, stop=False)
                return MM(dst, ll, rh, start=False, stop=stop)

            def x_transposes(t):
                pe.wait_ge(x_norm, t + 1)
                for hf in range(2):
                    n = 2 * t + hf
                    if n >= 4:
                        pe.wait_ge(hl_ready, n - 3)
                    for k in range(4):
                        ins = nc.tensor.transpose(xt[n % 4][:, k * P:(k + 1) * P], tiles(xtile(t), 4 * hf + k), ident)
                    ins.then_inc(xt_done, 1)

            def item(e, m):
                kind, _, w, _ = ENTRIES[e]
                n = first_item[e] + m
                if n >= 4:
                    pe.wait_ge(act_rel, releases[n - 4][0])
                    pe.wait_ge(dve_rel, releases[n - 4][1])
                bank = pj[n % 4]
                pe.wait_ge(hl_ready, 2 * m + 2 if kind in ("q", "kv") else 8 * (m % 2 + 1))
                for k in range(NK):
                    if m == 0 and k % 2 == 0:
                        pe.wait_ge(wh_ready, 4 * e + k // 2 + 1)
                        pe.wait_ge(wl_ready, 4 * e + k // 2 + 1)
                    if kind in ("q", "kv"):
                        s = slice(m * P, (m + 1) * P)
                        c = slice(k * w, (k + 1) * w)
                        ins = three(bank[:, 0:w], hh[:, k, s], hl[:, k, s], wh[e % 2][:, c], wl[e % 2][:, c],
                                    k == 0, k == NK - 1)
                    else:
                        f, hf = divmod(m, 2)
                        s = slice(hf * 512, (hf + 1) * 512)
                        c = slice(k * w + f * P, k * w + (f + 1) * P)
                        ins = three(bank[:, :], wh[e % 2][:, c], wl[e % 2][:, c], hh[:, k, s], hl[:, k, s],
                                    k == 0, k == NK - 1)
                ins.then_inc(item_done, 1)

            def hidden(e, f):
                pe.wait_ge(wh_ready, 4 * e + 4)
                pe.wait_ge(wl_ready, 4 * e + 4)
                pe.wait_ge(xcl_ready, f + 1)
                if f == 1:
                    pe.wait_ge(hid_pre, 1)
                for l in range(CMP_STRIDE):
                    c = slice(l * P, (l + 1) * P)
                    ins = three(xt[2][:, 0:P], wh[e % 2][:, c], wl[e % 2][:, c], xch[:, l, :], xcl[:, l, :],
                                l == 0, l == CMP_STRIDE - 1)
                ins.then_inc(hid_done, 1)

            def compressed(f):
                pe.wait_ge(hdl_ready, f + 1)
                pe.wait_ge(w2_ready, 1)
                if f == 1:
                    pe.wait_ge(ck_raw, 2)
                three(xt[3][:, 0:HD], hdh[:, :], hdl[:, :], w2h[:, f, :], w2l[:, f, :], True, True)\
                    .then_inc(cmp_done, 1)

            def key_transposes(n0, normed):
                pe.wait_ge(keys_normed, normed)
                for n in range(4):
                    g, hf = divmod(n, 2)
                    if n0 + n >= 2:
                        pe.wait_ge(kt_ready, n0 + n - 1)
                    for j in range(4):
                        kk = krow[:, 4 * hf + j, g].rearrange("p u d -> p (u d)")
                        ins = nc.tensor.transpose(xt[(n0 + n) % 2][:, j * P:(j + 1) * P], kk, ident)
                    ins.then_inc(kt_done, 1)

            pe.wait_ge(masks_ready, 1)
            for t in range(NT + 1):
                if t < NT:
                    x_transposes(t)
                if t >= 1:
                    item(0, t - 1)
            for e in range(1, NE):
                kind, _, _, idx = ENTRIES[e]
                for m in range(items_of(e)):
                    item(e, m)
                    if kind == "kv" and m == 2:
                        compressed(idx)
                    if kind == "kv" and idx == 1 and m == 1:
                        key_transposes(0, 1)
                if kind == "w1":
                    hidden(e, idx)
                if kind == "kv" and idx == 1:
                    pe.wait_ge(keys_normed, 2)
                    pe.wait_ge(kt_ready, 3)
                    nc.tensor.transpose(xt[0][:, 0:P], ckr.rearrange("p u d -> p (u d)"), ident).then_inc(kt_done, 1)
                if kind == "z" and idx == 0:
                    key_transposes(5, 3)

            wait_phase_a(pe)
            pe.wait_ge(kt_ready, 9)
            pe.wait_ge(cv_ready, 1)
            tpn = ptn = 0

            q_tp = {}

            def queries(u):
                nonlocal tpn
                pe.wait_ge(qd_ready, u + 1)
                if tpn >= 2:
                    pe.wait_ge(tp_read, tpn - 1)
                for h in range(GH):
                    ins = nc.tensor.transpose(tp[tpn % 2][:, h * P:(h + 1) * P],
                                              qd[:, h, :, :].rearrange("p u d -> p (u d)"), ident)
                ins.then_inc(tp_done, 1)
                tpn += 1
                q_tp[u] = tpn

            def keys_times(dst, keys, h, mask=None):
                MM(dst, qh[:, h, :], keys, start=True, stop=False)
                last = MM(dst, ql[:, h, :], keys, start=False, stop=not mask)
                for n, (cols, m) in enumerate(mask or []):
                    last = MM(cols, identr, m, start=False, stop=n == len(mask) - 1)
                return last

            def scores(w, h):
                i, g = UNITS[w // 2]
                k = 4 * w + h
                if h == 0 and w % 2 == 0:
                    pe.wait_ge(tp_read, q_tp[w // 2])
                if k >= 2:
                    pe.wait_ge(exp_done, k - 1)
                s = sc[k % 2]
                causal = masks[:, C_CAUSAL:C_CAUSAL + P]
                far = masks[:, C_FAR:C_FAR + P]
                if w % 2 == 0:
                    j0, n, br = 0, i + 1, 0
                else:
                    j0 = max(0, i - WT)
                    n, br = i + 1 - j0, 1
                for a in range(0, n, 4):
                    b = min(n, a + 4)
                    mask = []
                    if br == 1 and a == 0 and i >= WT:
                        mask.append((s[:, 0:P], far))
                    if b == n:
                        mask.append((s[:, (n - 1) * P:n * P], causal))
                    ins = keys_times(s[:, a * P:b * P], kst[:, br, g, (j0 + a) * P:(j0 + b) * P], h, mask)
                if br == 1:
                    c0 = C_CMP + (NT - 1) * 8 - 8 * i
                    ins = keys_times(s[:, 640:704], kcmp[:, g * CB:(g + 1) * CB], h, [(s[:, 640:704], masks[:, c0:c0 + CB])])
                ins.then_inc(s_done, 1)

            pending = None

            def flush():
                nonlocal pending
                if pending is None:
                    return
                n, (kind, j), pt, first, last = pending
                pending = None
                i, g = UNITS[n // 2]
                pe.wait_ge(tp_read, tp_of[pt])
                if first:
                    pe.wait_ge(o_read, n // 2) if n >= 2 else None
                v = vcmp[:, g, :] if kind == "c" else val[:, "sw".index(kind), j, g, :]
                r = CB if kind == "c" else P
                MM(po[:, :], v, pth[pt % 2][0:r, :], start=first, stop=False)
                MM(po[:, :], v, ptl[pt % 2][0:r, :], start=False, stop=last).then_inc(pv_done, 1)

            tp_of = {}

            def turn(n, kind, j):
                nonlocal tpn, ptn, pending
                i, g = UNITS[n // 2]
                if tpn >= 2:
                    pe.wait_ge(tp_read, tpn - 1)
                r = CB if kind == "c" else P
                for h in range(GH):
                    if kind == "s":
                        src = p_sel[:, h, j * P:(j + 1) * P]
                    elif kind == "w":
                        c = j - max(0, i - WT)
                        src = p_win[:, h, c * P:(c + 1) * P]
                    else:
                        src = p_win[:, h, 640:704]
                    ins = nc.tensor.transpose(tp[tpn % 2][0:r, h * P:(h + 1) * P], src, ident)
                ins.then_inc(tp_done, 1)
                tpn += 1
                tp_of[ptn] = tpn
                flush()
                pending = (n, (kind, j), ptn, n % 2 == 0 and j == 0, kind == "c")
                ptn += 1

            def output(i, part):
                n, k = divmod(part, 8)
                c = 2 * (NT - 1 - i) + n
                if part == 0:
                    pe.wait_ge(msl_ready, NT - i)
                    pe.wait_ge(wol_ready, NK)
                if k == 0 and c >= 1:
                    pe.wait_ge(out_ready, c)
                s = slice(n * 512, (n + 1) * 512)
                ins = three(pout[:, :], msh[:, k, :], msl[:, k, :], woh[:, k, s], wol[:, k, s], k == 0, k == NK - 1)
                if k == NK - 1:
                    ins.then_inc(out_done, 1)

            queries(0)
            for w in range(LAST_W + 1):
                for h in range(4):
                    if w < NJ:
                        scores(w, h)
                    u = q_prep_at(w, h)
                    if u is not None:
                        queries(u)
                    part = out_part(w, h)
                    if part is not None:
                        output(*part)
                    if 1 <= w <= NJ:
                        if h == 0:
                            pe.wait_ge(p_ready, 4 * w)
                        for kind, j in quarter(w - 1, h):
                            turn(w - 1, kind, j)
                flush()


def constants():
    c = np.zeros((P, NC_), np.float32)
    r, k = np.arange(P)[:, None], np.arange(P)[None, :]
    c[:, C_ID:C_ID + P] = r == k
    c[:, C_CAUSAL:C_CAUSAL + P] = np.where(k <= r, 0, NEG)
    c[:, C_FAR:C_FAR + P] = np.where(k > r, 0, NEG)
    a = np.arange(120)[None, :] - 8 * (NT - 1)
    c[:, C_CMP:C_CMP + 120] = np.where(CMP_STRIDE * a + CMP_LEN - 1 <= r, 0, NEG)
    freq = np.float32(500000.0) ** (-np.arange(0, 2 * ROT, 2, dtype=np.float32) / np.float32(2 * ROT))
    pos = (np.arange(NT)[None, :] * P + r).astype(np.float32)
    ang = pos[:, :, None] * freq
    c[:, C_COS:C_COS + 64] = np.cos(ang).reshape(P, -1)
    c[:, C_SIN:C_SIN + 64] = np.sin(ang).reshape(P, -1)
    end = ((np.arange(P) % CB) * CMP_STRIDE + CMP_LEN - 1).astype(np.float32)[:, None] * freq
    c[:, C_COSC:C_COSC + ROT], c[:, C_SINC:C_SINC + ROT] = np.cos(end), np.sin(end)
    c[:, C_VALID] = np.arange(P) >= CMP_LEN - 1
    c[:, C_EPS] = EPS
    return c


def kernel(x, norm_w, w_in, q_norm_w, k_norm_w, cmp_k_pos, cmp_k_w1, cmp_k_b1, cmp_k_w2,
           cmp_v_pos, cmp_v_w1, cmp_v_b1, cmp_v_w2, conv_w, conv_b, w_out):
    import concourse.bacc as bacc
    from concourse.bass_utils import run_bass_kernel_spmd as run

    a = lambda v: np.asarray(v)
    w3 = a(w_in)[0].reshape(NK, P, -1).transpose(1, 0, 2)
    w1 = [a(w)[0].reshape(2, 16, HD, P).transpose(0, 2, 1, 3).reshape(P, -1) for w in (cmp_k_w1, cmp_v_w1)]
    packed = [w1[idx] if kind == "w1" else w3[:, :, col:col + w].reshape(P, -1) for kind, col, w, idx in ENTRIES]
    pos = [a(v)[0].reshape(2, 16, HD).transpose(0, 2, 1).reshape(P, 16) for v in (cmp_k_pos, cmp_v_pos)]
    params = [a(conv_w)[0].reshape(3, 4, P).transpose(2, 1, 0).reshape(P, 12), a(conv_b)[0].reshape(4, P).T,
              a(cmp_k_b1)[0].reshape(P, 1), a(cmp_v_b1)[0].reshape(P, 1), *pos, a(cmp_k_w2)[0], a(cmp_v_w2)[0]]
    ins = {
        "x": a(x)[0], "wpack": np.concatenate(packed, 1), "wout": a(w_out)[0], "normw": a(norm_w),
        "qnorm": a(q_norm_w), "knorm": a(k_norm_w)[0], "par": np.concatenate(params, 1), "const": constants(),
    }
    nc = bacc.Bacc("TRN2", target_bir_lowering=False, num_devices=1)
    arrays = {f"in_{n}": np.ascontiguousarray(v) for n, v in ins.items()}
    args = [nc.dram_tensor(n, v.shape, mybir.dt.from_np(v.dtype), kind="ExternalInput").ap() for n, v in arrays.items()]
    out = nc.dram_tensor("out_0", (SEQ, DM), F32, kind="ExternalOutput").ap()
    hybrid_layer(nc, *args, out)
    r = run(nc, [arrays], core_ids=[0])
    return r.results[0]["out_0"].reshape(1, SEQ, DM)
```

```python
from contextlib import ExitStack

import numpy as np

import concourse.bass as bass
from concourse import mybir

F32 = mybir.dt.float32
F32R = mybir.dt.float32r
ALU = mybir.AluOpType
ACT = mybir.ActivationFunctionType
AX = mybir.AxisListType

P = 128
SEQ = 1024
DM = 1024
NT = SEQ // P
NK = DM // P
HD = 64
HEADS, GROUPS = 8, 2
GH = HEADS // GROUPS
ROT = 8
CMP_STRIDE, CMP_LEN = 16, 32
CB = SEQ // CMP_STRIDE
WIN = 512
WT = WIN // P
EPS = 1e-6
NEG = -1e30
assert SEQ // 64 <= 16, "every selection block is among the top 16"

ENTRIES = [("q", 0, 256, 0), ("kc", 512, 256, 0), ("q", 256, 256, 1), ("w1", 0, 256, 0),
           ("kv", 768, 256, 0), ("w1", 1, 256, 1), ("kv", 1024, 280, 1),
           ("z", 1304, 256, 0), ("z", 1560, 256, 1)]
for pair in range(2):
    for kind, col in (("ch", 1816), ("cc", 2840), ("cb", 2328), ("cz", 3352)):
        ENTRIES.append((kind, col + 256 * pair, 256, pair))
NE = len(ENTRIES)
ITEMS = {"q": NT, "kv": NT, "w1": 0}
OFFS = [0]
for _, _, w, _ in ENTRIES:
    OFFS.append(OFFS[-1] + NK * w)

C_ID, C_CAUSAL, C_FAR, C_CMP = 0, 128, 256, 384
C_COS, C_SIN, C_COSC, C_SINC, C_VALID, C_EPS, NC_ = 504, 568, 632, 640, 648, 649, 650
P_CW, P_CB, P_B1, P_POS, P_W2, NPAR = 0, 12, 16, 18, 50, 178


def items_of(e):
    return ITEMS.get(ENTRIES[e][0], 4)


UNITS = [(i, g) for i in reversed(range(NT)) for g in range(GROUPS)]
NJ = 2 * len(UNITS)
NS = 4 * NJ
ACT_HEADS = (0,)


def job_tiles(n):
    i, _ = UNITS[n // 2]
    if n % 2 == 0:
        return [("s", j) for j in range(i + 1)]
    return [("w", j) for j in range(max(0, i - WT), i + 1)] + [("c", 0)]


def turns_at(k):
    n, h = divmod(k - 5, 4)
    if not 0 <= n < NJ:
        return None, []
    t = job_tiles(n)
    return n, t[len(t) * h // 4:len(t) * (h + 1) // 4]


def unit_at(k, first, every=8):
    u, rest = divmod(k - first, every)
    return u if rest == 0 and 0 <= u < 8 * NT * 2 // every else None


def queries_at(k):
    u = unit_at(k, -2)
    return u or None


def output_at(k):
    return unit_at(k, 13)


PARTS = [(n, kt) for n in range(2) for kt in (4, 5, 6, 7, 0, 1, 2, 3)]
PART_0 = 23


def part_at(k):
    m, part = divmod(k - PART_0, len(PARTS))
    return (m, part) if 0 <= m < NT else (None, 0)


STEPS = PART_0 + len(PARTS) * NT


def transposes_until():
    tp, pt, at, pv = 1, 0, {}, {}
    for k in range(STEPS):
        n, t = turns_at(k)
        if n is not None:
            tp += len(t)
            pt += len(t)
            at[n], pv[n] = tp, pt
        if queries_at(k) is not None:
            tp += 1
    return at, pv


def hybrid_layer(nc: bass.Bass, x, wpack, wout, normw, qnorm, knorm, par, const, out):
    with ExitStack() as ctx:
        def sb(name, shape, dt=F32, c=ctx):
            return c.enter_context(nc.sbuf_tensor(name, shape, dt))

        cst = sb("cst", [P, NC_])
        masks = sb("masks", [P, 504], F32R)
        gate = sb("gate", [P, NT, 3 * HEADS])
        kcmp = sb("kcmp", [P, P], F32R)
        vcmp = sb("vcmp", [CB, GROUPS, P], F32R)
        nmax = sb("nmax", [P, 4, 2])
        psums = sb("psums", [P, 4, 2])
        precip = sb("precip", [P, 4, 2])
        qn = sb("qn", [P, NT, HEADS * HD])
        kst = sb("kst", [P, 2, GROUPS, SEQ], F32R)
        val = sb("val", [P, 2, NT, GROUPS, P], F32R)
        mixn = sb("mixn", [P, 4, SEQ])
        with ExitStack() as c:
            xch = sb("xch", [P, 16, P], F32R, c)
            xcl = sb("xcl", [P, 16, P], F32R, c)
        mixc = sb("mixc", [P, 4, SEQ])

        with ExitStack() as c:
            hh = sb("hh", [P, NK, SEQ], F32R, c)
            hl = sb("hl", [P, NK, SEQ], F32R, c)
            raw = [sb(f"raw{s}", [P, 560], F32, c) for s in range(4)]
            wh = [sb(f"wh{s}", [P, NK * (280 - 24 * s)], F32R, c) for s in range(2)]
            wl = [sb(f"wl{s}", [P, NK * (280 - 24 * s)], F32R, c) for s in range(2)]
            ub = sb("ub", [P, 2 * (SEQ + 2)], F32, c)
            sq = sb("sq", [P, 512], F32, c)
            hdh = sb("hdh", [P, P], F32R, c)
            hdl = sb("hdl", [P, P], F32R, c)
            prm = sb("prm", [P, NPAR], F32, c)
            hnorm = sb("hnorm", [P, 4, HD], F32, c)
            w2h = sb("w2h", [P, 2, HD], F32R, c)
            w2l = sb("w2l", [P, 2, HD], F32R, c)
            stat = sb("stat", [P, 5, 48], F32, c)
        with ExitStack() as c:
            woh = sb("woh", [P, NK, DM], F32R, c)
            wol = sb("wol", [P, NK, DM], F32R, c)
            p_sel = sb("p_sel", [P, GH, SEQ], F32, c)
            p_win = sb("p_win", [P, GH, 704], F32, c)
            pth = [sb(f"pth{s}", [P, 512], F32R, c) for s in range(2)]
            ptl = [sb(f"ptl{s}", [P, 512], F32R, c) for s in range(2)]
            qh = sb("qh", [P, GH, P], F32R, c)
            ql = sb("ql", [P, GH, P], F32R, c)
            qd = sb("qd", [P, GH, 2, HD], F32, c)
            ot = sb("ot", [P, 2, P], F32, c)
            xo = [sb(f"xo{s}", [P, 512], F32, c) for s in range(2)]
            with ExitStack() as d:
                wor = [sb(f"wor{s}", [P, DM], F32, d) for s in range(2)]
            msh = sb("msh", [P, NK, P], F32R, c)
            msl = sb("msl", [P, NK, P], F32R, c)

        with ExitStack() as c:
            pj = [c.enter_context(nc.psum_tensor(f"pj{s}", [P, 512], F32)) for s in range(4)]
            xt = [c.enter_context(nc.psum_tensor(f"xt{s}", [P, 512], F32)) for s in range(4)]
        with ExitStack() as c:
            sc = [c.enter_context(nc.psum_tensor(f"sc{s}", [P, 1024], F32)) for s in range(2)]
            tp = [c.enter_context(nc.psum_tensor(f"tp{s}", [P, 512], F32)) for s in range(2)]
            po = c.enter_context(nc.psum_tensor("po", [P, 512], F32))
            pout = c.enter_context(nc.psum_tensor("pout", [P, 512], F32))

        def sem(name):
            return ctx.enter_context(nc.semaphore(name))

        const_in, param_in, normw_in = sem("const_in"), sem("param_in"), sem("normw_in")
        x_in = [sem(f"x_in{s}") for s in range(2)]
        raw_in = [sem(f"raw_in{s}") for s in range(4)]
        scratch_set = sem("scratch_set")
        masks_ready, w2_hi, w2_ready = sem("masks_ready"), sem("w2_hi"), sem("w2_ready")
        x_sq, x_std, x_norm = sem("x_sq"), sem("x_std"), sem("x_norm")
        xt_done, hh_ready, hl_ready = sem("xt_done"), sem("hh_ready"), sem("hl_ready")
        wh_ready, wl_ready = sem("wh_ready"), sem("wl_ready")
        item_done, act_rel, dve_rel = sem("item_done"), sem("act_rel"), sem("dve_rel")
        sq_ready, sq_read = sem("sq_ready"), sem("sq_read")
        head_std = sem("head_std")
        th_ready, cz_done, q_normed = sem("th_ready"), sem("cz_done"), sem("q_normed")
        blocks_ready, xch_ready, xcl_ready = sem("blocks_ready"), sem("xch_ready"), sem("xcl_ready")
        hid_done, hid_pre, hid_tanh, hid_act = sem("hid_done"), sem("hid_pre"), sem("hid_tanh"), sem("hid_act")
        hdh_ready, hdl_ready, cmp_done = sem("hdh_ready"), sem("hdl_ready"), sem("cmp_done")
        ck_raw, ck_std, cv_hi, cv_ready = sem("ck_raw"), sem("ck_std"), sem("cv_hi"), sem("cv_ready")
        ck_sum = sem("ck_sum")
        keys_normed, kt_done, kt_hi, kt_ready = sem("keys_normed"), sem("kt_done"), sem("kt_hi"), sem("kt_ready")
        gate_raw, gate_tanh = sem("gate_raw"), sem("gate_tanh")
        dve_chain = sem("dve_chain")
        wor_in = [sem(f"wor_in{s}") for s in range(2)]
        woh_ready, wol_ready = sem("woh_ready"), sem("wol_ready")
        qd_ready, qh_ready = sem("qd_ready"), sem("qh_ready")
        s_done, max_ready, exp_done = sem("s_done"), sem("max_ready"), sem("exp_done")
        recip_ready, factor_ready = sem("recip_ready"), sem("factor_ready")
        p_act, p_dve, cmp_scaled = sem("p_act"), sem("p_dve"), sem("cmp_scaled")
        tp_done, tp_read, pth_ready = sem("tp_done"), sem("tp_read"), sem("pth_ready")
        pv_done, ot_copied, o_read, mix_ready = sem("pv_done"), sem("ot_copied"), sem("o_read"), sem("mix_ready")
        msh_ready, msl_ready = sem("msh_ready"), sem("msl_ready")
        out_done, out_ready, mixc_used = sem("out_done"), sem("out_ready"), sem("mixc_used")
        xo_in = [sem(f"xo_in{s}") for s in range(2)]
        stored = [sem(f"stored{s}") for s in range(2)]

        ident = cst[:, C_ID:C_ID + P]
        identr = masks[:, C_ID:C_ID + P]
        tiles = lambda ap, t: ap[:, t * P:(t + 1) * P]
        xtile = lambda t: ub[:, (t % 2) * SEQ:(t % 2 + 1) * SEQ]
        krow = ub[:, 0:SEQ * 2].rearrange("p (t g u d) -> p t g u d", t=NT, g=GROUPS, u=2)
        ubuf = ub[:, :].rearrange("p (f s) -> p f s", f=2)
        blocks = [mixn[:, 2 * f:2 * f + 2, :] for f in range(2)]
        hid = mixn[:, 0, 0:4 * P].rearrange("p (a c) -> p a c", a=4)
        ckr = mixn[:, 1, 0:2 * HD].rearrange("p (u d) -> p u d", u=2)
        cksq = mixn[:, 1, 2 * HD:3 * HD]
        cktmp = mixn[:, 1, 256:288].rearrange("p (a r) -> p a r", a=4)
        tp_end, pv_end = transposes_until()
        first_item = [sum(items_of(a) for a in range(e)) for e in range(NE + 1)]
        releases, ra, rd = [], 0, 0
        kind_of = [kind for kind, *_ in ENTRIES for _ in range(ITEMS.get(kind, 4))]
        for kind, *_ in ENTRIES:
            for _ in range(ITEMS.get(kind, 4)):
                ra += kind in ("q", "kv", "kc", "ch")
                rd += kind in ("kv", "kc", "z", "cc", "cb", "cz")
                releases.append((ra, rd))

        def entry_through(eng, e):
            if ENTRIES[e][0] == "w1":
                eng.wait_ge(hid_done, ENTRIES[e][3] + 1)
            else:
                eng.wait_ge(item_done, first_item[e + 1])

        def gate_of(s, branch):
            i, g = UNITS[s // 8]
            c = 3 * (GH * g + s % 4) + branch
            return gate[:, i, c:c + 1]

        def main_probs(s):
            i, _ = UNITS[s // 8]
            if s // 4 % 2 == 0:
                return p_sel[:, s % 4, 0:(i + 1) * P]
            return p_win[:, s % 4, 0:(min(i, WT) + 1) * P]

        def wait_phase_a(eng):
            entry_through(eng, NE - 1)
            eng.wait_ge(th_ready, kind_of.count("z") + kind_of.count("cz"))
            eng.wait_ge(cz_done, kind_of.count("cz"))

        def wait_last_entry(eng):
            entry_through(eng, NE - 2)

        block = ctx.enter_context(nc.Block())

        @block.sync
        def _(sp):
            sp.dma_start(xtile(0), x[0:P, :]).then_inc(x_in[0], 16)
            sp.dma_start(cst[:, :], const).then_inc(const_in, 16)
            sp.dma_start(mixc[:, 0, :], normw.to_broadcast([P, DM])).then_inc(normw_in, 16)
            sp.dma_start(xtile(1), x[P:2 * P, :]).then_inc(x_in[1], 16)

            def weights(p):
                e, j = divmod(p, 4)
                w = 2 * ENTRIES[e][2]
                if p >= 4:
                    sp.wait_ge(wh_ready, p - 3)
                    sp.wait_ge(wl_ready, p - 3)
                sp.dma_start(raw[p % 4][:, 0:w], wpack[:, OFFS[e] + j * w:OFFS[e] + (j + 1) * w])\
                    .then_inc(raw_in[p % 4], 16)

            for p in range(4):
                weights(p)
            sp.dma_start(prm[:, :], par).then_inc(param_in, 16)
            sp.dma_start(hnorm[:, 0, :], qnorm.to_broadcast([P, HD])).then_inc(param_in, 16)
            for b in range(3):
                sp.dma_start(hnorm[:, 1 + b, :], knorm[b:b + 1, :].to_broadcast([P, HD])).then_inc(param_in, 16)
            for t in range(2, NT):
                sp.wait_ge(xt_done, 2 * (t - 2) + 2)
                sp.dma_start(xtile(t), x[t * P:(t + 1) * P, :]).then_inc(x_in[t % 2], 16)
                if t == 4:
                    for p in range(4, 8):
                        weights(p)
            for p in range(8, 4 * NE):
                weights(p)

            wait_phase_a(sp)

            def residual(c):
                i, n = NT - 1 - c // 2, c % 2
                sp.dma_start(xo[c % 2][:, :], x[i * P:(i + 1) * P, n * 512:(n + 1) * 512]).then_inc(xo_in[c % 2], 16)

            for k in range(NK):
                if k >= 2:
                    sp.wait_ge(woh_ready, k - 1)
                    sp.wait_ge(wol_ready, k - 1)
                sp.dma_start(wor[k % 2][:, :], wout[k * P:(k + 1) * P, :]).then_inc(wor_in[k % 2], 16)
            for c in range(2):
                residual(c)
            for c in range(2 * NT):
                i, n = NT - 1 - c // 2, c % 2
                sp.wait_ge(out_ready, c + 1)
                sp.dma_start(out[i * P:(i + 1) * P, n * 512:(n + 1) * 512], xo[c % 2][:, :]).then_inc(stored[c % 2], 16)
                if c + 2 < 2 * NT:
                    sp.wait_ge(stored[c % 2], 16 * (c // 2 + 1))
                    residual(c + 2)
            for s in range(2):
                sp.wait_ge(stored[s], 16 * NT)

        @block.gpsimd
        def _(pool):
            def weights(p):
                e, j = divmod(p, 4)
                w = 2 * ENTRIES[e][2]
                pool.wait_ge(wh_ready, p + 1)
                nc.gpsimd.tensor_tensor(wl[e % 2][:, j * w:(j + 1) * w], raw[p % 4][:, 0:w],
                                        wh[e % 2][:, j * w:(j + 1) * w].bitcast(F32), ALU.subtract)\
                    .then_inc(wl_ready, 1)

            def block_lo(f):
                pool.wait_ge(xch_ready, f + 1)
                v = blocks[f].rearrange("p g (c l) -> p l g c", l=CMP_STRIDE)
                o = xcl[:, :, :].rearrange("p l (g c) -> p l g c", g=GROUPS)
                hi = xch[:, :, :].rearrange("p l (g c) -> p l g c", g=GROUPS).bitcast(F32)
                if f == 1:
                    pool.wait_ge(hid_done, 1)
                for g in range(GROUPS):
                    ins = nc.gpsimd.tensor_tensor(o[:, :, g], v[:, :, g], hi[:, :, g], ALU.subtract)
                ins.then_inc(xcl_ready, 1)

            for e in range(NE):
                for j in range(4):
                    weights(4 * e + j)
                if e == 2:
                    block_lo(0)
                if e == 4:
                    block_lo(1)
            def copy_queries(u):
                i, g = UNITS[u]
                if u >= 1:
                    pool.wait_ge(qh_ready, u)
                src = qn[:, i, g * 256:(g + 1) * 256].rearrange("p (h d) -> p h d", h=GH)
                for twice in range(2):
                    ins = nc.gpsimd.tensor_copy(qd[:, :, twice, :], src)
                ins.then_inc(qd_ready, 1)

            wait_last_entry(pool)
            pool.wait_ge(q_normed, 2)
            copy_queries(0)
            wait_phase_a(pool)

            for k in range(STEPS):
                if k % 2 == 1 and k < 2 * NK:
                    p = k // 2
                    pool.wait_ge(woh_ready, p + 1)
                    nc.gpsimd.tensor_tensor(wol[:, p, :], wor[p % 2][:, :], woh[:, p, :].bitcast(F32), ALU.subtract)\
                        .then_inc(wol_ready, 1)
                s = k - 1
                if 0 <= s < NS and s // 4 % 2 == 1:
                    pool.wait_ge(recip_ready, s + 1)
                    p = p_win[:, s % 4, 640:704]
                    nc.gpsimd.tensor_scalar(p, p, precip[:, s % 4, 1:2], gate_of(s, 0), ALU.mult, ALU.mult)\
                        .then_inc(cmp_scaled, 1)
                if unit_at(k, -6):
                    copy_queries(unit_at(k, -6))
                for first, half, mix in ((PART_0 - 4, 4, mixc), (PART_0, 0, mixn)):
                    m = unit_at(k, first, 16)
                    if m is not None:
                        pool.wait_ge(msh_ready, 2 * m + (2 if half == 0 else 1))
                        nc.gpsimd.tensor_tensor(msl[:, half:half + 4, :], mix[:, :, (NT - 1 - m) * P:(NT - m) * P],
                                                msh[:, half:half + 4, :].bitcast(F32), ALU.subtract).then_inc(msl_ready, 1)

        @block.scalar
        def _(act):
            A = nc.scalar.activation

            def weights(p):
                e, j = divmod(p, 4)
                if e >= NE:
                    return
                w = 2 * ENTRIES[e][2]
                act.wait_ge(raw_in[p % 4], 16 * (p // 4 + 1))
                if e >= 2:
                    entry_through(act, e - 2)
                nc.scalar.copy(wh[e % 2][:, j * w:(j + 1) * w], raw[p % 4][:, 0:w]).then_inc(wh_ready, 1)

            def item(e, m):
                kind, _, _, idx = ENTRIES[e]
                n = first_item[e] + m
                bank = pj[n % 4]
                act.wait_ge(item_done, n + 1)
                if kind in ("q", "kv"):
                    tk = n - sum(items_of(a) for a in range(e) if ENTRIES[a][0] not in ("q", "kv"))
                    w = 256 if kind == "q" else 128
                    if tk >= 2:
                        act.wait_ge(sq_read, tk - 1)
                    A(sq[:, (tk % 2) * 256:(tk % 2) * 256 + w], bank[:, 0:w], ACT.Square).then_inc(sq_ready, 1)
                    if kind == "q":
                        nc.scalar.copy(qn[:, m, idx * 256:(idx + 1) * 256], bank[:, 0:256]).then_inc(act_rel, 1)
                    else:
                        if idx == 1 and m == 0:
                            act.wait_ge(kt_done, 4)
                        if idx == 0 and m == 0:
                            act.wait_ge(q_normed, 2)
                        nc.scalar.copy(krow[:, m, :, 0, :], bank[:, 0:128].rearrange("p (g d) -> p g d", g=GROUPS))
                        nc.scalar.copy(val[:, idx, m, :, 0:HD],
                                       bank[:, 128:256].rearrange("p (g d) -> p g d", g=GROUPS)).then_inc(act_rel, 1)
                elif kind == "kc":
                    f, hf = divmod(m, 2)
                    if m == 0:
                        act.wait_ge(x_norm, NT)
                    o, s = (0, 16) if hf == 0 else (496, 0)
                    nc.scalar.copy(blocks[f][0:HD, 0, hf * 512:(hf + 1) * 512], bank[0:HD, :])
                    nc.scalar.copy(blocks[f][HD:P, 0, o:o + 512 - s], bank[0:HD, s:512]).then_inc(act_rel, 1)
                elif kind in ("z", "cz"):
                    before = [i for i in range(n) if kind_of[i] in ("z", "cz")]
                    if not before:
                        act.wait_ge(sq_read, 32)
                    elif kind_of[before[-1]] == "z":
                        act.wait_ge(dve_rel, releases[before[-1]][1])
                    else:
                        act.wait_ge(cz_done, kind_of[:n].count("cz"))
                    A(sq[:, :], bank[:, :], ACT.Tanh, scale=0.5).then_inc(th_ready, 1)
                elif kind == "ch":
                    f, hf = divmod(m, 2)
                    nc.scalar.copy(mixc[:, 2 * idx + f, hf * 512:(hf + 1) * 512], bank[:, :]).then_inc(act_rel, 1)

            def key_hi(n, dst, width=512):
                act.wait_ge(kt_done, n + 1)
                nc.scalar.copy(dst, xt[n % 2][:, 0:width]).then_inc(kt_hi, 1)

            def hidden(f):
                act.wait_ge(hid_pre, f + 1)
                A(hid[:, 1], hid[:, 0], ACT.Tanh, scale=0.5).then_inc(hid_tanh, 1)
                act.wait_ge(hid_act, f + 1)
                if f == 1:
                    act.wait_ge(cmp_done, 1)
                A(hdh[:, :], hid[:, 2], ACT.Copy, scale=0.5).then_inc(hdh_ready, 1)

            def block_hi(f):
                act.wait_ge(blocks_ready, f + 1)
                if f == 1:
                    act.wait_ge(hid_done, 1)
                v = blocks[f].rearrange("p g (c l) -> p l g c", l=CMP_STRIDE)
                o = xch[:, :, :].rearrange("p l (g c) -> p l g c", g=GROUPS)
                for g in range(GROUPS):
                    ins = nc.scalar.copy(o[:, :, g], v[:, :, g])
                ins.then_inc(xch_ready, 1)

            act.wait_ge(scratch_set, 1)
            A(stat[:, 1, 47:48], stat[:, 0, 47:48], ACT.Sqrt)
            act.wait_ge(const_in, 16)
            for t in range(NT + 2):
                if t < NT:
                    act.wait_ge(x_in[t % 2], 16 * (t // 2 + 1))
                    A(kst[:, :, :, :].rearrange("p b g s -> p (b g s)")[:, (t % 4) * SEQ:(t % 4 + 1) * SEQ],
                      xtile(t), ACT.Square, accum_out=stat[:, 0, 32 + t:33 + t]).then_inc(x_sq, 1)
                    act.wait_ge(x_sq, t + 1)
                    A(stat[:, 1, 32 + t:33 + t], stat[:, 0, 32 + t:33 + t], ACT.Sqrt, scale=1.0 / DM,
                      bias=cst[:, C_EPS:C_EPS + 1]).then_inc(x_std, 1)
                    if t == 2:
                        nc.scalar.copy(masks[:, :], cst[:, 0:504]).then_inc(masks_ready, 1)
                    for p in {0: (0, 1), 1: (2, 3), 2: (), 3: ()}.get(t, (t,)):
                        weights(p)
                if 1 <= t <= NT:
                    for hf in range(2):
                        act.wait_ge(xt_done, 2 * (t - 1) + hf + 1)
                        nc.scalar.copy(hh[:, 4 * hf:4 * hf + 4, (t - 1) * P:t * P],
                                       xt[(2 * (t - 1) + hf) % 4][:, :].rearrange("p (k s) -> p k s", k=4))\
                            .then_inc(hh_ready, 1)
                if t >= 2:
                    item(0, t - 2)
            act.wait_ge(param_in, 80)
            nc.scalar.copy(w2h[:, :, :], prm[:, P_W2:P_W2 + 128].rearrange("p (f d) -> p f d", f=2)).then_inc(w2_hi, 1)

            norms = 0

            def root(count, scale=1.0 / HD):
                nonlocal norms
                norms += 1
                act.wait_ge(sq_read, 8 * norms)
                A(stat[:, 1, 0:count], stat[:, 0, 0:count], ACT.Sqrt, scale=scale,
                  bias=cst[:, C_EPS:C_EPS + 1]).then_inc(head_std, 1)

            tpn = ptn = 0

            def queries(u):
                nonlocal tpn
                act.wait_ge(tp_done, tpn + 1)
                if u >= 1:
                    act.wait_ge(s_done, 8 * u)
                nc.scalar.copy(qh[:, :, :], tp[tpn % 2][:, :].rearrange("p (h q) -> p h q", h=GH)).then_inc(qh_ready, 1)
                tpn += 1

            root(32)
            for e in range(1, NE):
                kind, _, _, idx = ENTRIES[e]
                if kind == "kv" and idx == 1:
                    for n in range(4):
                        key_hi(n, kst[:, 0, n // 2, (n % 2) * 512:(n % 2 + 1) * 512])
                for m in range(items_of(e)):
                    item(e, m)
                    if m < 4:
                        weights(4 * (e + 1) + m)
                    if e == NE - 1 and m == 2:
                        queries(0)
                if kind == "w1":
                    for j in range(4):
                        weights(4 * (e + 1) + j)
                    hidden(idx)
                    if idx == 0:
                        block_hi(1)
                    else:
                        act.wait_ge(cmp_done, 1)
                        A(cksq, xt[3][:, 0:HD], ACT.Square).then_inc(ck_raw, 1)
                        nc.scalar.copy(ckr[:, 0, :], xt[3][:, 0:HD]).then_inc(ck_raw, 1)
                        act.wait_ge(ck_sum, 1)
                        A(stat[:, 1, 16:17], stat[:, 0, 16:17], ACT.Sqrt, scale=1.0 / HD,
                          bias=cst[:, C_EPS:C_EPS + 1]).then_inc(ck_std, 1)
                if kind == "kc":
                    block_hi(0)
                if kind == "q":
                    root(32)
                if kind == "kv":
                    root(16)
                    if idx == 1:
                        key_hi(4, kcmp[:, :], P)
                        act.wait_ge(cmp_done, 2)
                        for g in range(GROUPS):
                            ins = nc.scalar.copy(vcmp[:, g, 0:HD], xt[3][g * HD:(g + 1) * HD, 0:HD])
                        ins.then_inc(cv_hi, 1)
                        act.wait_ge(gate_raw, NT)
                        A(gate[:, :, :], gate[:, :, :], ACT.Tanh, scale=0.5).then_inc(gate_tanh, 1)
                if kind == "z" and idx == 0:
                    for n in range(4):
                        key_hi(5 + n, kst[:, 1, n // 2, (n % 2) * 512:(n % 2 + 1) * 512])

            wait_phase_a(act)
            def exponentials(s):
                w, h = divmod(s, 4)
                i, g = UNITS[w // 2]
                act.wait_ge(max_ready, s + 1)
                if h == 0 and w >= 2:
                    act.wait_ge(tp_done, tp_end[w - 2])
                if w % 2 == 0:
                    A(p_sel[:, h, 0:(i + 1) * P], sc[s % 2][:, 0:(i + 1) * P], ACT.Exp,
                      bias=nmax[:, s % 4, 0:1], accum_out=psums[:, s % 4, 0:1]).then_inc(exp_done, 1)
                else:
                    n = min(i, WT) + 1
                    A(p_win[:, h, 640:704], sc[s % 2][:, 640:704], ACT.Exp,
                      bias=nmax[:, s % 4, 1:2], accum_out=psums[:, s % 4, 1:2])
                    A(p_win[:, h, 0:n * P], sc[s % 2][:, 0:n * P], ACT.Exp,
                      bias=nmax[:, s % 4, 0:1], accum_out=psums[:, s % 4, 0:1]).then_inc(exp_done, 1)

            def prob_hi(kind):
                nonlocal tpn, ptn
                r = CB if kind == "c" else P
                act.wait_ge(tp_done, tpn + 1)
                if ptn >= 2:
                    act.wait_ge(pv_done, ptn - 1)
                nc.scalar.copy(pth[ptn % 2][0:r, :], tp[tpn % 2][0:r, :]).then_inc(pth_ready, 1)
                tpn += 1
                ptn += 1

            for k in range(STEPS):
                _, turned = turns_at(k)
                if 1 <= k <= NS:
                    exponentials(k - 1)
                for kind, _ in turned[:1]:
                    prob_hi(kind)
                u = output_at(k)
                if u is not None:
                    act.wait_ge(pv_done, pv_end[2 * u + 1])
                    if u >= 1:
                        act.wait_ge(mix_ready, u)
                    o4 = po[:, :].rearrange("p (a b q) -> p a b q", a=2, b=2)
                    nc.scalar.copy(ot[0:HD, :, :], o4[HD:P, :, 0, :])
                    nc.scalar.copy(ot[HD:P, :, :], o4[0:HD, :, 1, :]).then_inc(ot_copied, 1)
                for kind, _ in turned[1:]:
                    prob_hi(kind)
                s = k - 2
                if 0 <= s < NS and s % 4 in ACT_HEADS:
                    act.wait_ge(factor_ready, len(ACT_HEADS) * (s // 4) + ACT_HEADS.index(s % 4) + 1)
                    A(main_probs(s), main_probs(s), ACT.Copy, scale=precip[:, s % 4, 0:1]).then_inc(p_act, 1)
                if k % 2 == 1 and k < 2 * NK:
                    p = k // 2
                    act.wait_ge(wor_in[p % 2], 16 * (p // 2 + 1))
                    nc.scalar.copy(woh[:, p, :], wor[p % 2][:, :]).then_inc(woh_ready, 1)
                m = unit_at(k, PART_0 - 4, 16)
                if m is not None:
                    act.wait_ge(wol_ready, NK)
                    act.wait_ge(mixc_used, m)
                    nc.scalar.copy(msh[:, 4:8, :], mixc[:, :, (NT - 1 - m) * P:(NT - m) * P]).then_inc(msh_ready, 1)
                m = unit_at(k, PART_0, 16)
                if m is not None:
                    act.wait_ge(mix_ready, 2 * m + 2)
                    act.wait_ge(out_done, 2 * m)
                    nc.scalar.copy(msh[:, 0:4, :], mixn[:, :, (NT - 1 - m) * P:(NT - m) * P]).then_inc(msh_ready, 1)
                if queries_at(k) is not None:
                    queries(queries_at(k))

        @block.vector
        def _(dve):
            V = nc.vector
            chain = 0

            def link(ins):
                nonlocal chain
                chain += 1
                ins.then_inc(dve_chain, 1)
                dve.wait_ge(dve_chain, chain)

            def inv_std(lo, n, width, ready, count):
                s = lambda r: stat[:, r, lo:lo + n]
                dve.wait_ge(ready, count)
                V.tensor_scalar(s(3), s(0), 1.0 / width, EPS, ALU.mult, ALU.add)
                link(V.reciprocal(s(2), s(1)))
                link(V.tensor_tensor(s(4), s(2), s(2), ALU.mult))
                link(V.scalar_tensor_tensor(s(4), s(4), -0.5, s(3), ALU.mult, ALU.mult))
                link(V.scalar_tensor_tensor(s(2), s(4), 1.5, s(2), ALU.add, ALU.mult))

            def rope(v, cos, sin, tmp):
                a, b = v[..., 0:ROT], v[..., ROT:2 * ROT]
                V.tensor_tensor(tmp[0], a, cos, ALU.mult)
                V.tensor_tensor(tmp[1], b, sin, ALU.mult)
                V.tensor_tensor(tmp[2], b, cos, ALU.mult)
                link(V.tensor_tensor(tmp[3], a, sin, ALU.mult))
                V.tensor_tensor(a, tmp[0], tmp[1], ALU.subtract)
                return V.tensor_tensor(b, tmp[2], tmp[3], ALU.add)

            def item(e, m):
                kind, _, _, idx = ENTRIES[e]
                n = first_item[e] + m
                bank = pj[n % 4]
                if kind in ("q", "kv"):
                    tk = n - sum(items_of(a) for a in range(e) if ENTRIES[a][0] not in ("q", "kv"))
                    nh = 4 if kind == "q" else 2
                    dve.wait_ge(sq_ready, tk + 1)
                    V.tensor_reduce(stat[:, 0, m * nh:(m + 1) * nh],
                                    sq[:, (tk % 2) * 256:(tk % 2) * 256 + nh * HD].rearrange("p (h d) -> p h d", h=nh),
                                    AX.X, ALU.add).then_inc(sq_read, 1)
                    if kind == "kv":
                        dve.wait_ge(act_rel, releases[n][0])
                        if idx == 1:
                            V.tensor_copy(gate[:, m, :], bank[:, 256:280]).then_inc(gate_raw, 1)
                        V.tensor_tensor(val[:, idx, m, :, HD:P], bank[:, 128:256].rearrange("p (g d) -> p g d", g=GROUPS),
                                        val[:, idx, m, :, 0:HD].bitcast(F32), ALU.subtract).then_inc(dve_rel, 1)
                    return
                dve.wait_ge(item_done, n + 1)
                f, hf = divmod(m, 2)
                cols = slice(hf * 512, (hf + 1) * 512)
                if kind == "kc":
                    o, s = (0, 16) if hf == 0 else (496, 0)
                    V.tensor_copy(blocks[f][0:HD, 1, cols], bank[HD:P, :])
                    V.tensor_copy(blocks[f][HD:P, 1, o:o + 512 - s], bank[HD:P, s:512]).then_inc(dve_rel, 1)
                elif kind == "z":
                    zi = sum(k in ("z", "cz") for k in kind_of[:n])
                    dve.wait_ge(th_ready, zi + 1)
                    V.scalar_tensor_tensor(mixn[:, 2 * idx + f, cols], sq[:, :], 1.0, bank[:, :], ALU.add, ALU.mult)\
                        .then_inc(dve_rel, 1)
                elif kind == "cc":
                    dve.wait_ge(act_rel, releases[n][0])
                    V.tensor_tensor(ubuf[:, f, 2 + hf * 512:2 + (hf + 1) * 512], bank[:, :],
                                    mixc[:, 2 * idx + f, cols], ALU.mult).then_inc(dve_rel, 1)
                    dve.wait_ge(dve_rel, releases[n][1])
                    if hf == 1:
                        t = 2 * idx + f
                        y = mixc[:, t, :]
                        cw = lambda k: prm[:, P_CW + 3 * t + k:P_CW + 3 * t + k + 1]
                        link(V.tensor_scalar(y, ubuf[:, f, 2:2 + SEQ], cw(2), prm[:, P_CB + t:P_CB + t + 1],
                                             ALU.mult, ALU.add))
                        link(V.scalar_tensor_tensor(y, ubuf[:, f, 1:1 + SEQ], cw(1), y, ALU.mult, ALU.add))
                        link(V.scalar_tensor_tensor(y, ubuf[:, f, 0:SEQ], cw(0), y, ALU.mult, ALU.add))
                elif kind == "cb":
                    mc = mixc[:, 2 * idx + f, cols]
                    V.tensor_tensor(mc, bank[:, :], mc, ALU.mult).then_inc(dve_rel, 1)
                elif kind == "cz":
                    zi = sum(k in ("z", "cz") for k in kind_of[:n])
                    dve.wait_ge(th_ready, zi + 1)
                    mc = mixc[:, 2 * idx + f, cols]
                    V.scalar_tensor_tensor(sq[:, :], sq[:, :], 1.0, bank[:, :], ALU.add, ALU.mult).then_inc(dve_rel, 1)
                    dve.wait_ge(dve_rel, releases[n][1])
                    V.scalar_tensor_tensor(mc, sq[:, :], 0.5, mc, ALU.mult, ALU.mult).then_inc(cz_done, 1)

            def key_lo(n, dst, width=512):
                dve.wait_ge(kt_hi, n + 1)
                V.tensor_tensor(dst, xt[n % 2][HD:P, 0:width], dst.bitcast(F32), ALU.subtract).then_inc(kt_ready, 1)

            V.memset(stat[:, 0, 47:48], 1.0).then_inc(scratch_set, 1)
            dve.wait_ge(normw_in, 16)
            dve.wait_ge(const_in, 16)
            for t in range(NT + 2):
                if t < NT:
                    inv_std(32 + t, 1, DM, x_std, t + 1)
                    V.scalar_tensor_tensor(xtile(t), xtile(t), stat[:, 2, 32 + t:33 + t], mixc[:, 0, :], ALU.mult, ALU.mult)\
                        .then_inc(x_norm, 1)
                if 1 <= t <= NT:
                    for hf in range(2):
                        n = 2 * (t - 1) + hf
                        dve.wait_ge(hh_ready, n + 1)
                        hi = hh[:, 4 * hf:4 * hf + 4, (t - 1) * P:t * P]
                        V.tensor_tensor(hl[:, 4 * hf:4 * hf + 4, (t - 1) * P:t * P],
                                        xt[n % 4][:, :].rearrange("p (k s) -> p k s", k=4), hi.bitcast(F32),
                                        ALU.subtract).then_inc(hl_ready, 1)
                if t >= 2:
                    item(0, t - 2)
            dve.wait_ge(w2_hi, 1)
            V.tensor_tensor(w2l[:, :, :], prm[:, P_W2:P_W2 + 128].rearrange("p (f d) -> p f d", f=2),
                            w2h[:, :, :].bitcast(F32), ALU.subtract).then_inc(w2_ready, 1)
            link(V.tensor_scalar(hnorm[:, 0, :], hnorm[:, 0, :], 0.125, None, ALU.mult))
            cos = cst[:, C_COS:C_COS + 64].rearrange("p (t r) -> p t r", t=NT)
            sin = cst[:, C_SIN:C_SIN + 64].rearrange("p (t r) -> p t r", t=NT)
            norms = 0

            def normalise(v, nh, weight, tmp):
                nonlocal norms
                norms += 1
                inv_std(0, NT * nh, HD, head_std, norms)
                r = stat[:, 2, 0:NT * nh].rearrange("p (t h) -> p t h", t=NT)
                wide = [P, NT, nh, HD]
                link(V.tensor_tensor(v, v, r.unsqueeze(3).to_broadcast(wide), ALU.mult))
                link(V.tensor_tensor(v, v, hnorm[:, weight, :].unsqueeze(1).unsqueeze(1).to_broadcast(wide), ALU.mult))
                some = [P, NT, nh, ROT]
                return rope(v, cos.unsqueeze(2).to_broadcast(some), sin.unsqueeze(2).to_broadcast(some), tmp)

            def normalise_q(idx):
                v = qn[:, :, idx * 256:(idx + 1) * 256].rearrange("p t (h d) -> p t h d", h=4)
                tmp = [ub[:, 256 * k:256 * (k + 1)].rearrange("p (t h r) -> p t h r", t=NT, h=4) for k in range(4)]
                normalise(v, 4, 0, tmp).then_inc(q_normed, 1)
                dve.wait_ge(q_normed, idx + 1)

            tpn = ptn = 0

            def queries(u):
                nonlocal tpn
                dve.wait_ge(qh_ready, u + 1)
                V.tensor_tensor(ql[:, :, :], tp[tpn % 2][:, :].rearrange("p (h q) -> p h q", h=GH),
                                qh[:, :, :].bitcast(F32), ALU.subtract).then_inc(tp_read, 1)
                tpn += 1

            normalise_q(0)
            for e in range(1, NE):
                kind, _, _, idx = ENTRIES[e]
                if kind == "kv" and idx == 1:
                    for n in range(4):
                        key_lo(n, kst[HD:P, 0, n // 2, (n % 2) * 512:(n % 2 + 1) * 512])
                if kind == "kc":
                    for f in range(2):
                        for g in range(GROUPS):
                            link(V.memset(blocks[f][HD:P, g, SEQ - 16:SEQ], 0.0))
                if kind == "ch" and idx == 0:
                    for f in range(2):
                        link(V.memset(ubuf[:, f, 0:2], 0.0))
                if kind != "ch":
                    for m in range(items_of(e)):
                        item(e, m)
                        if e == NE - 1 and m == 2:
                            queries(0)
                if kind == "kc":
                    dve.wait_ge(dve_rel, 4)
                    for f in range(2):
                        dve.wait_ge(act_rel, 8 + 2 * f + 2)
                        for g in range(GROUPS):
                            v = blocks[f][:, g, :].rearrange("p (c l) -> p c l", l=CMP_STRIDE)
                            pos = prm[:, P_POS + 16 * f:P_POS + 16 * (f + 1)].unsqueeze(1).to_broadcast([P, CB, CMP_STRIDE])
                            ins = V.tensor_tensor(v, v, pos, ALU.add)
                        ins.then_inc(blocks_ready, 1)
                if kind == "q":
                    normalise_q(idx)
                if kind == "w1":
                    dve.wait_ge(hid_done, idx + 1)
                    dve.wait_ge(xcl_ready, idx + 1)
                    V.tensor_scalar(hid[:, 0], xt[2][:, 0:P], prm[:, P_B1 + idx:P_B1 + idx + 1], None, ALU.add)\
                        .then_inc(hid_pre, 1)
                    dve.wait_ge(hid_tanh, idx + 1)
                    V.scalar_tensor_tensor(hid[:, 2], hid[:, 1], 1.0, hid[:, 0], ALU.add, ALU.mult).then_inc(hid_act, 1)
                    dve.wait_ge(hdh_ready, idx + 1)
                    V.scalar_tensor_tensor(hdl[:, :], hid[:, 2], 0.5, hdh[:, :].bitcast(F32), ALU.mult, ALU.subtract)\
                        .then_inc(hdl_ready, 1)
                    if idx == 1:
                        dve.wait_ge(ck_raw, 2)
                        V.tensor_reduce(stat[:, 0, 16:17], cksq, AX.X, ALU.add).then_inc(ck_sum, 1)
                        inv_std(16, 1, HD, ck_std, 1)
                        c = ckr[:, 0, :]
                        link(V.scalar_tensor_tensor(c, c, stat[:, 2, 16:17], hnorm[:, 1, :], ALU.mult, ALU.mult))
                        link(rope(c, cst[:, C_COSC:C_COSC + ROT], cst[:, C_SINC:C_SINC + ROT],
                                  [cktmp[:, k, :] for k in range(4)]))
                        V.tensor_copy(ckr[:, 1, :], c).then_inc(keys_normed, 1)
                if kind == "kv":
                    v = krow[:, :, :, 0, :]
                    tmp = [krow[:, :, :, 1, ROT * k:ROT * (k + 1)] for k in range(4)]
                    link(normalise(v, 2, 2 + idx, tmp))
                    for g in range(GROUPS):
                        ins = V.tensor_copy(krow[:, :, g, 1, :], krow[:, :, g, 0, :])
                    ins.then_inc(keys_normed, 1)
                    if idx == 1:
                        key_lo(4, kcmp[HD:P, :], P)
                        dve.wait_ge(cv_hi, 1)
                        for g in range(GROUPS):
                            ins = V.tensor_tensor(vcmp[:, g, HD:P], xt[3][g * HD:(g + 1) * HD, 0:HD],
                                                  vcmp[:, g, 0:HD].bitcast(F32), ALU.subtract)
                        ins.then_inc(cv_ready, 1)
                        dve.wait_ge(gate_tanh, 1)
                        link(V.tensor_scalar(gate[:, :, :], gate[:, :, :], 0.5, 0.5, ALU.mult, ALU.add))
                        g0 = gate[:, 0, :].rearrange("p (h b) -> p h b", b=3)[:, :, 0]
                        link(V.tensor_scalar(g0, g0, cst[:, C_VALID:C_VALID + 1], None, ALU.mult))
                if kind == "z" and idx == 0:
                    for n in range(4):
                        key_lo(5 + n, kst[HD:P, 1, n // 2, (n % 2) * 512:(n % 2 + 1) * 512])

            wait_phase_a(dve)

            def scale(s):
                w, h = divmod(s, 4)
                i, g = UNITS[w // 2]
                b = w % 2
                main = gate_of(s, 2 if b else 1)
                factor = precip[:, s % 4, 0:1]
                if b and w >= 3:
                    dve.wait_ge(cmp_scaled, 4 * (w // 2))
                dve.wait_ge(exp_done, s + 1)
                V.reciprocal(precip[:, s % 4, 0:1 + b], psums[:, s % 4, 0:1 + b]).then_inc(recip_ready, 1)
                dve.wait_ge(recip_ready, s + 1)
                if h in ACT_HEADS:
                    V.tensor_tensor(factor, factor, main, ALU.mult).then_inc(factor_ready, 1)
                else:
                    p = main_probs(s)
                    V.tensor_scalar(p, p, factor, main, ALU.mult, ALU.mult).then_inc(p_dve, 1)

            def maxima(s):
                w, _ = divmod(s, 4)
                i, g = UNITS[w // 2]
                dve.wait_ge(s_done, s + 1)
                if w % 2 == 0:
                    V.tensor_reduce(nmax[:, s % 4, 0:1], sc[s % 2][:, 0:(i + 1) * P], AX.X, ALU.max,
                                    negate=True).then_inc(max_ready, 1)
                else:
                    V.tensor_reduce(nmax[:, s % 4, 1:2], sc[s % 2][:, 640:704], AX.X, ALU.max, negate=True)
                    V.tensor_reduce(nmax[:, s % 4, 0:1], sc[s % 2][:, 0:(min(i, WT) + 1) * P], AX.X, ALU.max,
                                    negate=True).then_inc(max_ready, 1)

            def prob_lo(kind):
                nonlocal tpn, ptn
                r = CB if kind == "c" else P
                dve.wait_ge(pth_ready, ptn + 1)
                V.tensor_tensor(ptl[ptn % 2][0:r, :], tp[tpn % 2][0:r, :], pth[ptn % 2][0:r, :].bitcast(F32),
                                ALU.subtract).then_inc(tp_read, 1)
                tpn += 1
                ptn += 1

            for k in range(STEPS):
                if k < NS:
                    maxima(k)
                _, turned = turns_at(k)
                for kind, _ in turned[:1]:
                    prob_lo(kind)
                if 1 <= k <= NS:
                    scale(k - 1)
                u = output_at(k)
                if u is not None:
                    i, g = UNITS[u]
                    o4 = po[:, :].rearrange("p (a b q) -> p a b q", a=2, b=2)
                    dve.wait_ge(ot_copied, u + 1)
                    V.tensor_tensor(ot[0:HD, :, :], o4[0:HD, :, 0, :], ot[0:HD, :, :], ALU.add)
                    V.tensor_tensor(ot[HD:P, :, :], o4[HD:P, :, 1, :], ot[HD:P, :, :], ALU.add).then_inc(o_read, 1)
                    dve.wait_ge(o_read, u + 1)
                    mx = mixn[:, 2 * g:2 * g + 2, i * P:(i + 1) * P]
                    V.scalar_tensor_tensor(mx, mx, 0.5, ot[:, :, :], ALU.mult, ALU.mult).then_inc(mix_ready, 1)
                m, part = part_at(k)
                if m is not None and part % 8 == 7:
                    c = 2 * m + part // 8
                    dve.wait_ge(out_done, c + 1)
                    dve.wait_ge(xo_in[c % 2], 16 * (c // 2 + 1))
                    V.tensor_tensor(xo[c % 2][:, :], pout[:, :], xo[c % 2][:, :], ALU.add).then_inc(out_ready, 1)
                for kind, _ in turned[1:]:
                    prob_lo(kind)
                if queries_at(k) is not None:
                    queries(queries_at(k))

        @block.tensor
        def _(pe):
            MM = nc.tensor.matmul

            def three(dst, lh, ll, rh, rl, start, stop):
                MM(dst, lh, rh, start=start, stop=False)
                MM(dst, lh, rl, start=False, stop=False)
                return MM(dst, ll, rh, start=False, stop=stop)

            def x_transposes(t):
                pe.wait_ge(x_norm, t + 1)
                for hf in range(2):
                    n = 2 * t + hf
                    if n >= 4:
                        pe.wait_ge(hl_ready, n - 3)
                    for k in range(4):
                        ins = nc.tensor.transpose(xt[n % 4][:, k * P:(k + 1) * P], tiles(xtile(t), 4 * hf + k), ident)
                    ins.then_inc(xt_done, 1)

            def item(e, m):
                kind, _, w, _ = ENTRIES[e]
                n = first_item[e] + m
                if n >= 4:
                    pe.wait_ge(act_rel, releases[n - 4][0])
                    pe.wait_ge(dve_rel, releases[n - 4][1])
                bank = pj[n % 4]
                pe.wait_ge(hl_ready, 2 * m + 2 if kind in ("q", "kv") else 8 * (m % 2 + 1))
                for k in range(NK):
                    if m == 0 and k % 2 == 0:
                        pe.wait_ge(wh_ready, 4 * e + k // 2 + 1)
                        pe.wait_ge(wl_ready, 4 * e + k // 2 + 1)
                    if kind in ("q", "kv"):
                        s = slice(m * P, (m + 1) * P)
                        c = slice(k * w, (k + 1) * w)
                        ins = three(bank[:, 0:w], hh[:, k, s], hl[:, k, s], wh[e % 2][:, c], wl[e % 2][:, c],
                                    k == 0, k == NK - 1)
                    else:
                        f, hf = divmod(m, 2)
                        s = slice(hf * 512, (hf + 1) * 512)
                        c = slice(k * w + f * P, k * w + (f + 1) * P)
                        ins = three(bank[:, :], wh[e % 2][:, c], wl[e % 2][:, c], hh[:, k, s], hl[:, k, s],
                                    k == 0, k == NK - 1)
                ins.then_inc(item_done, 1)

            def hidden(e, f):
                pe.wait_ge(wh_ready, 4 * e + 4)
                pe.wait_ge(wl_ready, 4 * e + 4)
                pe.wait_ge(xcl_ready, f + 1)
                if f == 1:
                    pe.wait_ge(hid_pre, 1)
                for l in range(CMP_STRIDE):
                    c = slice(l * P, (l + 1) * P)
                    ins = three(xt[2][:, 0:P], wh[e % 2][:, c], wl[e % 2][:, c], xch[:, l, :], xcl[:, l, :],
                                l == 0, l == CMP_STRIDE - 1)
                ins.then_inc(hid_done, 1)

            def compressed(f):
                pe.wait_ge(hdl_ready, f + 1)
                pe.wait_ge(w2_ready, 1)
                if f == 1:
                    pe.wait_ge(ck_raw, 2)
                three(xt[3][:, 0:HD], hdh[:, :], hdl[:, :], w2h[:, f, :], w2l[:, f, :], True, True)\
                    .then_inc(cmp_done, 1)

            def key_transposes(n0, normed):
                pe.wait_ge(keys_normed, normed)
                for n in range(4):
                    g, hf = divmod(n, 2)
                    if n0 + n >= 2:
                        pe.wait_ge(kt_ready, n0 + n - 1)
                    for j in range(4):
                        kk = krow[:, 4 * hf + j, g].rearrange("p u d -> p (u d)")
                        ins = nc.tensor.transpose(xt[(n0 + n) % 2][:, j * P:(j + 1) * P], kk, ident)
                    ins.then_inc(kt_done, 1)

            tpn = ptn = 0
            q_tp = {}

            def queries(u):
                nonlocal tpn
                pe.wait_ge(qd_ready, u + 1)
                if tpn >= 2:
                    pe.wait_ge(tp_read, tpn - 1)
                for h in range(GH):
                    ins = nc.tensor.transpose(tp[tpn % 2][:, h * P:(h + 1) * P],
                                              qd[:, h, :, :].rearrange("p u d -> p (u d)"), ident)
                ins.then_inc(tp_done, 1)
                tpn += 1
                q_tp[u] = tpn

            def keys_times(dst, keys, h, mask=None):
                MM(dst, qh[:, h, :], keys, start=True, stop=False)
                last = MM(dst, ql[:, h, :], keys, start=False, stop=not mask)
                for n, (cols, m) in enumerate(mask or []):
                    last = MM(cols, identr, m, start=False, stop=n == len(mask) - 1)
                return last

            def scores(k):
                w, h = divmod(k, 4)
                i, g = UNITS[w // 2]
                if h == 0 and w % 2 == 0:
                    pe.wait_ge(tp_read, q_tp[w // 2])
                if k >= 2:
                    pe.wait_ge(exp_done, k - 1)
                s = sc[k % 2]
                causal = masks[:, C_CAUSAL:C_CAUSAL + P]
                far = masks[:, C_FAR:C_FAR + P]
                if w % 2 == 0:
                    j0, n, br = 0, i + 1, 0
                else:
                    j0 = max(0, i - WT)
                    n, br = i + 1 - j0, 1
                for a in range(0, n, 4):
                    b = min(n, a + 4)
                    mask = []
                    if br == 1 and a == 0 and i >= WT:
                        mask.append((s[:, 0:P], far))
                    if b == n:
                        mask.append((s[:, (n - 1) * P:n * P], causal))
                    ins = keys_times(s[:, a * P:b * P], kst[:, br, g, (j0 + a) * P:(j0 + b) * P], h, mask)
                if br == 1:
                    c0 = C_CMP + (NT - 1) * 8 - 8 * i
                    ins = keys_times(s[:, 640:704], kcmp[:, g * CB:(g + 1) * CB], h, [(s[:, 640:704], masks[:, c0:c0 + CB])])
                ins.then_inc(s_done, 1)

            pe.wait_ge(const_in, 16)
            for t in range(NT + 1):
                if t < NT:
                    x_transposes(t)
                if t >= 1:
                    item(0, t - 1)
            for e in range(1, NE):
                kind, _, _, idx = ENTRIES[e]
                for m in range(items_of(e)):
                    item(e, m)
                    if kind == "kv" and m == 2:
                        compressed(idx)
                    if e == NE - 1 and m == 1:
                        pe.wait_ge(kt_ready, 9)
                        queries(0)
                    if kind == "kv" and idx == 1 and m == 1:
                        key_transposes(0, 1)
                if kind == "w1":
                    hidden(e, idx)
                if kind == "kv" and idx == 1:
                    pe.wait_ge(keys_normed, 2)
                    pe.wait_ge(kt_ready, 3)
                    nc.tensor.transpose(xt[0][:, 0:P], ckr.rearrange("p u d -> p (u d)"), ident).then_inc(kt_done, 1)
                if kind == "z" and idx == 0:
                    key_transposes(5, 3)

            pe.wait_ge(dve_rel, releases[first_item[NE - 1] + 1][1])
            pe.wait_ge(masks_ready, 1)
            scores(0)
            wait_phase_a(pe)
            pe.wait_ge(cv_ready, 1)
            pending = None

            def flush():
                nonlocal pending
                if pending is None:
                    return
                n, (kind, j), pt, first, last = pending
                pending = None
                i, g = UNITS[n // 2]
                pe.wait_ge(tp_read, tp_of[pt])
                if first and n >= 2:
                    pe.wait_ge(o_read, n // 2)
                v = vcmp[:, g, :] if kind == "c" else val[:, "sw".index(kind), j, g, :]
                r = CB if kind == "c" else P
                MM(po[:, :], v, pth[pt % 2][0:r, :], start=first, stop=False)
                MM(po[:, :], v, ptl[pt % 2][0:r, :], start=False, stop=last).then_inc(pv_done, 1)

            tp_of = {}

            def turn(n, kind, j):
                nonlocal tpn, ptn, pending
                i, g = UNITS[n // 2]
                if tpn >= 2:
                    pe.wait_ge(tp_read, tpn - 1)
                r = CB if kind == "c" else P
                for h in range(GH):
                    if kind == "s":
                        src = p_sel[:, h, j * P:(j + 1) * P]
                    elif kind == "w":
                        c = j - max(0, i - WT)
                        src = p_win[:, h, c * P:(c + 1) * P]
                    else:
                        src = p_win[:, h, 640:704]
                    ins = nc.tensor.transpose(tp[tpn % 2][0:r, h * P:(h + 1) * P], src, ident)
                ins.then_inc(tp_done, 1)
                tpn += 1
                tp_of[ptn] = tpn
                flush()
                pending = (n, (kind, j), ptn, n % 2 == 0 and j == 0, kind == "c")
                ptn += 1

            def output(m, part):
                n, k = PARTS[part]
                c = 2 * m + n
                if part == 0:
                    pe.wait_ge(wol_ready, NK)
                    pe.wait_ge(msl_ready, 2 * m + 1)
                if part == 4:
                    pe.wait_ge(msl_ready, 2 * m + 2)
                if part % 8 == 0 and c >= 1:
                    pe.wait_ge(out_ready, c)
                s = slice(n * 512, (n + 1) * 512)
                ins = three(pout[:, :], msh[:, k, :], msl[:, k, :], woh[:, k, s], wol[:, k, s],
                            part % 8 == 0, part % 8 == 7)
                if part % 8 == 7:
                    ins.then_inc(out_done, 1)
                if part == 11:
                    ins.then_inc(mixc_used, 1)

            for k in range(STEPS):
                n, turned = turns_at(k)
                if turned:
                    pe.wait_ge(p_act, len(ACT_HEADS) * (n + 1))
                    pe.wait_ge(p_dve, (GH - len(ACT_HEADS)) * (n + 1))
                    if n % 2 == 1:
                        pe.wait_ge(cmp_scaled, 4 * (n // 2 + 1))
                    turn(n, *turned[0])
                else:
                    flush()
                m, part = part_at(k)
                if m is not None:
                    output(m, part)
                for t in turned[1:]:
                    turn(n, *t)
                if k + 1 < NS:
                    scores(k + 1)
                if queries_at(k) is not None:
                    queries(queries_at(k))


def constants():
    c = np.zeros((P, NC_), np.float32)
    r, k = np.arange(P)[:, None], np.arange(P)[None, :]
    c[:, C_ID:C_ID + P] = r == k
    c[:, C_CAUSAL:C_CAUSAL + P] = np.where(k <= r, 0, NEG)
    c[:, C_FAR:C_FAR + P] = np.where(k > r, 0, NEG)
    a = np.arange(120)[None, :] - 8 * (NT - 1)
    c[:, C_CMP:C_CMP + 120] = np.where(CMP_STRIDE * a + CMP_LEN - 1 <= r, 0, NEG)
    freq = np.float32(500000.0) ** (-np.arange(0, 2 * ROT, 2, dtype=np.float32) / np.float32(2 * ROT))
    pos = (np.arange(NT)[None, :] * P + r).astype(np.float32)
    ang = pos[:, :, None] * freq
    c[:, C_COS:C_COS + 64] = np.cos(ang).reshape(P, -1)
    c[:, C_SIN:C_SIN + 64] = np.sin(ang).reshape(P, -1)
    end = ((np.arange(P) % CB) * CMP_STRIDE + CMP_LEN - 1).astype(np.float32)[:, None] * freq
    c[:, C_COSC:C_COSC + ROT], c[:, C_SINC:C_SINC + ROT] = np.cos(end), np.sin(end)
    c[:, C_VALID] = np.arange(P) >= CMP_LEN - 1
    c[:, C_EPS] = EPS
    return c


def kernel(x, norm_w, w_in, q_norm_w, k_norm_w, cmp_k_pos, cmp_k_w1, cmp_k_b1, cmp_k_w2,
           cmp_v_pos, cmp_v_w1, cmp_v_b1, cmp_v_w2, conv_w, conv_b, w_out):
    import concourse.bacc as bacc
    from concourse.bass_utils import run_bass_kernel_spmd as run

    a = lambda v: np.asarray(v)
    w3 = a(w_in)[0].reshape(NK, P, -1).transpose(1, 0, 2)
    w1 = [a(w)[0].reshape(2, 16, HD, P).transpose(0, 2, 1, 3).reshape(P, -1) for w in (cmp_k_w1, cmp_v_w1)]
    packed = [w1[idx] if kind == "w1" else w3[:, :, col:col + w].reshape(P, -1) for kind, col, w, idx in ENTRIES]
    pos = [a(v)[0].reshape(2, 16, HD).transpose(0, 2, 1).reshape(P, 16) for v in (cmp_k_pos, cmp_v_pos)]
    params = [a(conv_w)[0].reshape(3, 4, P).transpose(2, 1, 0).reshape(P, 12), a(conv_b)[0].reshape(4, P).T,
              a(cmp_k_b1)[0].reshape(P, 1), a(cmp_v_b1)[0].reshape(P, 1), *pos, a(cmp_k_w2)[0], a(cmp_v_w2)[0]]
    ins = {
        "x": a(x)[0], "wpack": np.concatenate(packed, 1), "wout": a(w_out)[0], "normw": a(norm_w),
        "qnorm": a(q_norm_w), "knorm": a(k_norm_w)[0], "par": np.concatenate(params, 1), "const": constants(),
    }
    nc = bacc.Bacc("TRN2", target_bir_lowering=False, num_devices=1)
    arrays = {f"in_{n}": np.ascontiguousarray(v) for n, v in ins.items()}
    args = [nc.dram_tensor(n, v.shape, mybir.dt.from_np(v.dtype), kind="ExternalInput").ap() for n, v in arrays.items()]
    out = nc.dram_tensor("out_0", (SEQ, DM), F32, kind="ExternalOutput").ap()
    hybrid_layer(nc, *args, out)
    r = run(nc, [arrays], core_ids=[0])
    return r.results[0]["out_0"].reshape(1, SEQ, DM)
```
